# Optimizing a Trainium2 kernel written in Bass

```python
import math
import jax, jax.numpy as jnp
from jax import lax
import numpy as np

D_MODEL = 2048
BATCH = 1
SEQ = 512
DEPTH = 2

N_MIXERS = 2
N_ATTN_LAYERS = (DEPTH + 1) // 2
N_LRU_LAYERS = DEPTH // 2

HEAD_DIM = 64
N_HEADS = D_MODEL // HEAD_DIM
N_KV_HEADS = N_HEADS // 8
GROUP = N_HEADS // N_KV_HEADS
WINDOW = 128
BLOCK = 128
Q_W = N_HEADS * HEAD_DIM
KV_W = N_KV_HEADS * HEAD_DIM
ATTN_IN_W = Q_W + 2 * KV_W + Q_W

LRU_W = D_MODEL
LRU_BLOCK_W = 256
N_LRU_BLOCKS = LRU_W // LRU_BLOCK_W
CONV_W = 4
C_RG = 8.0
LRU_IN_W = 2 * LRU_W

NORM_EPS = 1e-6
MASK_VALUE = -1e30

kernel_name = "hybrid_swa_sink_rglru_interleaved"

def rms_norm(x, g):
    x32 = x.astype(jnp.float32)
    y = x32 * lax.rsqrt(jnp.mean(x32 * x32, axis=-1, keepdims=True) + NORM_EPS)
    return (y * g.astype(jnp.float32)).astype(x.dtype)

def sliding_window_attention(h, w_in, w_out, sinks):
    B, S, _ = h.shape
    nb = S // BLOCK
    proj = h @ w_in
    q, k, v, gate = jnp.split(proj, [Q_W, Q_W + KV_W, Q_W + 2 * KV_W], axis=-1)
    q = q.reshape(B, nb, BLOCK, N_KV_HEADS, GROUP, HEAD_DIM)
    k = k.reshape(B, nb, BLOCK, N_KV_HEADS, HEAD_DIM)
    v = v.reshape(B, nb, BLOCK, N_KV_HEADS, HEAD_DIM)
    pad = ((0, 0), (1, 0), (0, 0), (0, 0), (0, 0))
    k_band = jnp.concatenate([jnp.pad(k, pad)[:, :-1], k], axis=2)
    v_band = jnp.concatenate([jnp.pad(v, pad)[:, :-1], v], axis=2)

    scale = 1.0 / math.sqrt(HEAD_DIM)
    scores = jnp.einsum('bnqkgd,bnskd->bnkgqs', q.astype(jnp.float32),
                        k_band.astype(jnp.float32)) * scale
    q_pos = jnp.arange(BLOCK)[:, None] + BLOCK
    k_pos = jnp.arange(2 * BLOCK)[None, :]
    rel = q_pos - k_pos
    in_window = (rel >= 0) & (rel < WINDOW)
    prev_exists = (jnp.arange(nb)[:, None, None] > 0) | (k_pos[None] >= BLOCK)
    mask = (in_window[None] & prev_exists)[:, None, None]
    scores = jnp.where(mask, scores, MASK_VALUE)

    sink = jnp.broadcast_to(
        sinks.astype(jnp.float32).reshape(1, 1, N_KV_HEADS, GROUP, 1, 1),
        scores.shape[:-1] + (1,))
    probs = jax.nn.softmax(jnp.concatenate([scores, sink], axis=-1), axis=-1)[..., :-1]
    out = jnp.einsum('bnkgqs,bnskd->bnqkgd', probs.astype(v.dtype), v_band)
    out = out.reshape(B, S, Q_W)
    return (out * jax.nn.silu(gate)) @ w_out

def _linear_combine(left, right):
    a1, b1 = left
    a2, b2 = right
    return a1 * a2, a2 * b1 + b2

def rglru_block(h, w_in, conv_w, conv_b, w_a, b_a, w_x, b_x, lam, w_out):
    B, S, _ = h.shape
    proj = h @ w_in
    xb, gate = jnp.split(proj, [LRU_W], axis=-1)
    xp = jnp.pad(xb, ((0, 0), (CONV_W - 1, 0), (0, 0)))
    xc = conv_b + sum(conv_w[tap] * xp[:, tap:tap + S] for tap in range(CONV_W))

    xg = xc.reshape(B, S, N_LRU_BLOCKS, LRU_BLOCK_W)
    r = jax.nn.sigmoid(jnp.einsum('bshi,hij->bshj', xg, w_a) + b_a).reshape(B, S, LRU_W)
    i = jax.nn.sigmoid(jnp.einsum('bshi,hij->bshj', xg, w_x) + b_x).reshape(B, S, LRU_W)

    log_a = -C_RG * r.astype(jnp.float32) * jax.nn.softplus(-lam.astype(jnp.float32))
    a = jnp.exp(log_a)
    mult = jnp.sqrt(-jnp.expm1(2.0 * log_a))
    b = mult * (i * xc).astype(jnp.float32)
    _, hs = lax.associative_scan(_linear_combine, (a, b), axis=1)
    y = hs.astype(h.dtype) * jax.nn.silu(gate)
    return y @ w_out

def setup_inputs(seed: int = 0) -> dict:
    key = jax.random.key(seed)
    ks = jax.random.split(key, 16)
    f32 = jnp.float32
    nrm = lambda k, shape, fan_in: jax.random.normal(k, shape, f32) * (fan_in ** -0.5)
    x = jax.random.normal(ks[0], (BATCH, SEQ, D_MODEL), f32)
    norm_pre = 1.0 + 0.05 * jax.random.normal(ks[1], (DEPTH, D_MODEL), f32)
    norm_post = 1.0 + 0.05 * jax.random.normal(ks[2], (DEPTH, D_MODEL), f32)

    attn_w_in = nrm(ks[3], (N_ATTN_LAYERS, D_MODEL, ATTN_IN_W), D_MODEL)
    attn_w_out = nrm(ks[4], (N_ATTN_LAYERS, Q_W, D_MODEL), Q_W)
    attn_sinks = 0.5 * jax.random.normal(ks[5], (N_ATTN_LAYERS, N_HEADS), f32)

    lru_w_in = nrm(ks[6], (N_LRU_LAYERS, D_MODEL, LRU_IN_W), D_MODEL)
    lru_conv_w = nrm(ks[7], (N_LRU_LAYERS, CONV_W, LRU_W), CONV_W)
    lru_conv_b = 0.01 * jax.random.normal(ks[8], (N_LRU_LAYERS, LRU_W), f32)
    lru_w_a = nrm(ks[9], (N_LRU_LAYERS, N_LRU_BLOCKS, LRU_BLOCK_W, LRU_BLOCK_W), LRU_BLOCK_W)
    lru_b_a = 0.01 * jax.random.normal(ks[10], (N_LRU_LAYERS, N_LRU_BLOCKS, LRU_BLOCK_W), f32)
    lru_w_x = nrm(ks[11], (N_LRU_LAYERS, N_LRU_BLOCKS, LRU_BLOCK_W, LRU_BLOCK_W), LRU_BLOCK_W)
    lru_b_x = 0.01 * jax.random.normal(ks[12], (N_LRU_LAYERS, N_LRU_BLOCKS, LRU_BLOCK_W), f32)
    u = jax.random.uniform(ks[13], (N_LRU_LAYERS, LRU_W), f32, 0.9, 0.999)
    a0 = u ** (1.0 / C_RG)
    lru_lambda = jnp.log(a0) - jnp.log1p(-a0)
    lru_w_out = nrm(ks[14], (N_LRU_LAYERS, LRU_W, D_MODEL), LRU_W)
    return {
        "x": x, "norm_pre": norm_pre, "norm_post": norm_post,
        "attn_w_in": attn_w_in, "attn_w_out": attn_w_out, "attn_sinks": attn_sinks,
        "lru_w_in": lru_w_in, "lru_conv_w": lru_conv_w, "lru_conv_b": lru_conv_b,
        "lru_w_a": lru_w_a, "lru_b_a": lru_b_a, "lru_w_x": lru_w_x, "lru_b_x": lru_b_x,
        "lru_lambda": lru_lambda, "lru_w_out": lru_w_out,
    }

def reference(x, norm_pre, norm_post, attn_w_in, attn_w_out, attn_sinks,
              lru_w_in, lru_conv_w, lru_conv_b, lru_w_a, lru_b_a, lru_w_x, lru_b_x,
              lru_lambda, lru_w_out):
    h = x
    for layer in range(DEPTH):
        u = rms_norm(h, norm_pre[layer])
        j = layer // N_MIXERS
        if layer % N_MIXERS == 0:
            y = sliding_window_attention(u, attn_w_in[j], attn_w_out[j], attn_sinks[j])
        else:
            y = rglru_block(u, lru_w_in[j], lru_conv_w[j], lru_conv_b[j], lru_w_a[j],
                            lru_b_a[j], lru_w_x[j], lru_b_x[j], lru_lambda[j], lru_w_out[j])
        h = h + rms_norm(y, norm_post[layer])
    return h


_drawn_inputs = setup_inputs


def setup_inputs(seed=0):
    import zlib

    import numpy as np

    out = dict(_drawn_inputs(seed))
    spreads = {}
    factors = {'attn_sinks': 3.428, 'lru_b_a': 50.218, 'lru_b_x': 24.845}
    for name, (base, spread) in spreads.items():
        noise = np.random.default_rng([zlib.crc32(name.encode()), seed]).standard_normal(out[name].shape)
        drawn = base * np.exp(spread * noise) if base else spread * noise
        out[name] = __import__('jax').numpy.asarray(drawn.astype(out[name].dtype))
    for name, factor in factors.items():
        out[name] = (out[name] * factor).astype(out[name].dtype)
    return out
```

```python
from contextlib import ExitStack

import concourse.bass as bass
from concourse import mybir

F32 = mybir.dt.float32
F32R = mybir.dt.float32r
ALU = mybir.AluOpType
ACT = mybir.ActivationFunctionType
AX_X = mybir.AxisListType.X
ds = bass.ds

P = 128
SEQ = 512
D = 2048
KT = D // P
ST = SEQ // P
HEAD = 64
HEADS = D // HEAD
KV_HEADS = HEADS // 8
KV_W = KV_HEADS * HEAD
CHUNKS = D // 256
NB = SEQ // P
EPS = 1e-6
MASKED = -1e30
CONV = 4
LRU_BW = 256

DEPTH = 4
LRU_DEPTH = 3
U_K, U_V, U_Q = 0, 4, 8
U_ATT = 12
U_O1 = U_ATT + 8 * CHUNKS - 4
U_LRU = U_O1 + 40
U_O2 = U_LRU + 9 * CHUNKS
UNITS = U_O2 + 40

ATT_STEPS = {1: [("S", 0)], 3: [("S", 1)], 4: [("T", 0, 1)], 5: [("V", 0)], 6: [("S", 2)],
             7: [("T", 1, 0)], 8: [("T", 1, 1)], 9: [("V", 1), ("S", 3)], 10: [("T", 2, 0)],
             11: [("T", 2, 1)], 12: [("V", 2)], 13: [("T", 3, 0)], 14: [("T", 3, 1)], 15: [("V", 3)]}


def t_index(c, b, k):
    return 7 * c + (0 if b == 0 else 2 * b - 1 + k)


def depth(u):
    return DEPTH if u < U_LRU or u > U_O2 + 2 else LRU_DEPTH


def slot(u):
    return (u - U_LRU) % LRU_DEPTH if U_LRU <= u < U_O2 else u % DEPTH


def landed(u):
    n = 0
    for v in range(u + 1):
        if slot(v) == slot(u):
            n += 16
            if U_LRU <= v < U_O2 and (v - U_LRU) % 9 == 8:
                n += 16
    return n


def build(nc, x, norm_pre, norm_post, w_in, w_out, sinks, l_in, conv_w, conv_b, w_a, b_a, w_x, b_x,
          lam, l_out, out):
    ctx = ExitStack()
    with ctx:
        base = (nc.sbuf_base + 63) // 64 * 64
        cursor = [base]

        def place(name, shape, dt, at=None):
            size = 4
            for n in shape[1:]:
                size *= n
            if at is None:
                at = cursor[0]
                cursor[0] += (size + 31) // 32 * 32
            return nc.alloc_sbuf_tensor_at(name, shape, dt, offset=at)

        def sem(name):
            return ctx.enter_context(nc.semaphore(name))

        u_hi = place("u_hi", [P, KT, SEQ], F32R)
        u_lo = place("u_lo", [P, KT, SEQ], F32R)
        y_at = cursor[0]
        mix = place("mix", [P, KT, SEQ], F32)
        h_at = cursor[0]
        h = place("h", [P, ST, D], F32)
        raw_at = cursor[0]
        raw = place("raw", [P, DEPTH, 1024], F32)
        w_hi = place("w_hi", [P, DEPTH, 1024], F32R)
        w_lo = place("w_lo", [P, DEPTH, 1024], F32R)
        ident = place("ident", [P, P], F32)
        vec = place("vec", [P, P], F32)
        mask = place("mask", [P, 2 * P], F32)
        nsink = place("nsink", [P, HEADS], F32)
        eps = place("eps", [P, 1], F32)
        stat = place("stat", [P, 128], F32)
        soft = place("soft", [P, 6, KT], F32)
        sp4 = place("sp4", [P, KT], F32)
        row_max = place("row_max", [P, 2, 4], F32)
        shift = place("shift", [P, 2, 4], F32)
        sink_shift = place("sink_shift", [P, 2, 4], F32)
        row_sum = place("row_sum", [P, 2, 4], F32)
        sink_exp = place("sink_exp", [P, 2, 4], F32)
        denom = place("denom", [P, 2, 4], F32)
        t_at = (cursor[0] + 63) // 64 * 64
        assert t_at + 7 * 4096 <= nc.sbuf_usable_end, (t_at, nc.sbuf_usable_end)
        K = 1024
        gain_pre = place("gain_pre", [P, D], F32, y_at)
        un = place("un", [P, 2, D], F32, y_at + 8 * K)
        square = place("square", [P, D], F32, t_at)
        gain_post = place("gain_post", [P, D], F32, t_at + 8 * K)
        x_again = place("x_again", [P, D], F32, t_at + 16 * K)
        vec_rows = place("vec_rows", [P, P], F32, t_at + 24 * K)
        y2 = place("y2", [P, ST, D], F32, y_at)
        kc = place("kc", [P, KV_HEADS, SEQ], F32, h_at)
        probs = place("probs", [P, 2, 4, 2 * P], F32, h_at + 8 * K)
        kz_hi = place("kz_hi", [P, 2, SEQ], F32R, h_at + 16 * K)
        kz_lo = place("kz_lo", [P, 2, SEQ], F32R, h_at + 20 * K)
        pt_hi = place("pt_hi", [P, 2, SEQ], F32R, h_at + 24 * K)
        pt_lo = place("pt_lo", [P, 2, SEQ], F32R, h_at + 28 * K)
        q_hi = place("q_hi", [P, 2, SEQ], F32R, t_at)
        q_lo = place("q_lo", [P, 2, SEQ], F32R, t_at + 4 * K)
        gate = place("gate", [P, 2, SEQ], F32, t_at + 8 * K)
        v_hi = place("v_hi", [P, NB, P], F32R, t_at + 12 * K)
        v_lo = place("v_lo", [P, NB, P], F32R, t_at + 14 * K)
        vc = place("vc", [P, NB, KV_W], F32, t_at + 16 * K)
        xc = place("xc", [P, 2, SEQ], F32, t_at)
        xc_hi = place("xc_hi", [P, 2, SEQ], F32R, t_at + 4 * K)
        xc_lo = place("xc_lo", [P, 2, SEQ], F32R, t_at + 8 * K)
        rg = place("rg", [P, 2, SEQ], F32, t_at + 12 * K)
        bt = place("bt", [P, 2, SEQ], F32, t_at + 16 * K)
        ig = place("ig", [P, 2, SEQ], F32, t_at + 20 * K)
        decay = place("decay", [P, 2, SEQ], F32, t_at + 24 * K)
        lgate = place("lgate", [P, 2, SEQ], F32, raw_at + 3 * 4 * K)
        lgate_last = place("lgate_last", [P, 2, SEQ], F32, base + 14 * 2 * K)
        bank = [ctx.enter_context(nc.psum_tensor(f"bank{i}", [P, 512], F32)) for i in range(8)]

        x_landed = [sem(f"x_landed{i}") for i in range(ST)]
        small_landed = sem("small_landed")
        pre_landed = sem("pre_landed")
        pre2_landed = sem("pre2_landed")
        post_landed = sem("post_landed")
        again_landed = sem("again_landed")
        raw_landed = [sem(f"raw_landed{i}") for i in range(DEPTH)]
        hi_done = sem("hi_done")
        lo_done = sem("lo_done")
        weights_used = sem("weights_used")
        consts_ready = sem("consts_ready")
        kz_zero = sem("kz_zero")
        vec_turned = sem("vec_turned")
        vec_ready = sem("vec_ready")
        soft_step = sem("soft_step")
        soft_exp = sem("soft_exp")
        sq_done = sem("sq_done")
        root_done = sem("root_done")
        sum_done = sem("sum_done")
        rstd_done = sem("rstd_done")
        scaled_done = sem("scaled_done")
        h_ready = sem("h_ready")
        un_ready = sem("un_ready")
        u_turned = sem("u_turned")
        u_hi_done = sem("u_hi_done")
        u_lo_done = sem("u_lo_done")
        v_proj = sem("v_proj")
        k_kept = sem("k_kept")
        v_kept = sem("v_kept")
        q_proj = sem("q_proj")
        q_hi_done = sem("q_hi_done")
        q_lo_done = sem("q_lo_done")
        gate_proj = sem("gate_proj")
        gate_tanh = sem("gate_tanh")
        gate_ready = sem("gate_ready")
        kz_hi_done = sem("kz_hi_done")
        kz_lo_done = sem("kz_lo_done")
        v_hi_done = sem("v_hi_done")
        v_lo_done = sem("v_lo_done")
        scores_done = sem("scores_done")
        scores_masked = sem("scores_masked")
        max_done = sem("max_done")
        shift_done = sem("shift_done")
        sink_shift_done = sem("sink_shift_done")
        exp_done = sem("exp_done")
        denom_done = sem("denom_done")
        recip_done = sem("recip_done")
        probs_ready = sem("probs_ready")
        p_turned = sem("p_turned")
        pt_hi_done = sem("pt_hi_done")
        pt_lo_done = sem("pt_lo_done")
        pv_done = sem("pv_done")
        pv_read = sem("pv_read")
        mix_ready = sem("mix_ready")
        mix_hi = sem("mix_hi")
        mix_lo = sem("mix_lo")
        o_done = sem("o_done")
        o_copied = sem("o_copied")
        o_squared = sem("o_squared")
        xb_proj = sem("xb_proj")
        conv_begun = sem("conv_begun")
        conv_tap = sem("conv_tap")
        xc_hi_done = sem("xc_hi_done")
        xc_lo_done = sem("xc_lo_done")
        lgate_proj = sem("lgate_proj")
        lgate_tanh = sem("lgate_tanh")
        lgate_ready = sem("lgate_ready")
        ri_proj = sem("ri_proj")
        r_done = sem("r_done")
        i_done = sem("i_done")
        t_done = sem("t_done")
        root_t_done = sem("root_t_done")
        one_plus_t = sem("one_plus_t")
        q_recip = sem("q_recip")
        b_step = sem("b_step")
        a_done = sem("a_done")
        ix_done = sem("ix_done")
        scan_done = sem("scan_done")
        lmix_ready = sem("lmix_ready")
        stored = sem("stored")

        LAM, B_A, B_X, CONV_B, CONV_W = 0, 16, 32, 48, 64

        def w_unit(w, row0, kts, col0, cols):
            return w[ds(row0, kts * P), ds(col0, cols)].rearrange("(k p) n -> p k n", p=P)

        def bcast(ap, shape):
            return ap.to_broadcast(shape)

        block = ctx.enter_context(nc.Block())

        @block.sync
        def _(sp):
            def load(s, u, free_after, src, parts=1):
                if free_after is not None:
                    sp.wait_ge(lo_done, free_after)
                dst = raw[:, s, :].rearrange("p (k n) -> p k n", n=src[0].shape[2])
                at = 0
                for part in src:
                    k = part.shape[1]
                    sp.dma_start(dst[:, at:at + k, :], part).then_inc(raw_landed[s], 16)
                    at += k

            def free(u):
                return u - depth(u) + 1 if u >= depth(u) else None

            for st in range(ST):
                sp.dma_start(h[:, st, :], x[st * P:(st + 1) * P, :]).then_inc(x_landed[st], 16)
                if st == 0:
                    sp.dma_start(gain_pre[:], norm_pre[0:1, :].to_broadcast([P, D])).then_inc(pre_landed, 16)
            sp.dma_start(nsink[:], sinks.to_broadcast([P, HEADS])).then_inc(small_landed, 16)
            rows = [(lam, LAM, 1), (b_a, B_A, 1), (b_x, B_X, 1), (conv_b, CONV_B, 1), (conv_w, CONV_W, CONV)]
            for v, r0, n in rows:
                sp.dma_start(vec_rows[r0:r0 + n * KT, :], v).then_inc(small_landed, 16)
            for kind, u0, col0 in (("k", U_K, D), ("v", U_V, D + KV_W)):
                for j in range(4):
                    load(slot(u0 + j), u0 + j, free(u0 + j), [w_unit(w_in, j * 512, 4, col0, 256)])
            for j in range(4):
                load(slot(U_Q + j), U_Q + j, free(U_Q + j), [w_unit(w_in, j * 512, 4, 0, 256)])

            def att_units(i, last):
                g0 = D + 2 * KV_W
                for p in range(4 if last else 8):
                    u = U_ATT + 8 * i + p
                    src = w_unit(w_in, (p % 4) * 512, 4, g0 + 256 * i if p < 4 else 256 * i + 256, 256)
                    load(p % DEPTH, u, u - DEPTH + 1, [src])

            with sp.Fori(0, CHUNKS - 1) as i:
                att_units(i, False)
            att_units(CHUNKS - 1, True)

            def out_units(w, u0):
                def chunk(n, u0n, frees):
                    for p in range(8):
                        if isinstance(n, int) and n == 0 and p == 3 and u0 == U_O2:
                            sp.wait_ge(lmix_ready, CHUNKS - 1)
                        load(p % DEPTH, u0n + p, frees(p), [w_unit(w, p * 256, 2, 512 * n, 512)])
                chunk(0, u0, lambda p: free(u0 + p))
                with sp.Fori(1, 3) as n:
                    chunk(n, u0 + 8 * n, lambda p: u0 + 8 * n + p - DEPTH + 1)
                for half in range(2):
                    chunk(3, u0 + 24 + 8 * half, lambda p: free(u0 + 24 + 8 * half + p))

            out_units(w_out, U_O1)

            def lru_units(j, last):
                for p in range(5 if last else 9):
                    u = U_LRU + 4 + 9 * j + p
                    if p < 4:
                        src = [w_unit(l_in, p * 512, 4, D + 256 * j, 256)]
                    elif p == 4:
                        src = [w_unit(w_a, LRU_BW * j, 2, 0, 256), w_unit(w_x, LRU_BW * j, 2, 0, 256)]
                    else:
                        src = [w_unit(l_in, (p - 5) * 512, 4, 256 * j + 256, 256)]
                    load((4 + p) % LRU_DEPTH, u, u - LRU_DEPTH + 1, src)

            for j in range(4):
                load(slot(U_LRU + j), U_LRU + j, free(U_LRU + j), [w_unit(l_in, j * 512, 4, 0, 256)])
            with sp.Fori(0, CHUNKS - 1) as j:
                lru_units(j, False)
            lru_units(CHUNKS - 1, True)
            out_units(l_out, U_O2)

            for st in range(ST):
                sp.wait_ge(h_ready, ST + st + 1)
                sp.dma_start(out[st * P:(st + 1) * P, :], h[:, st, :]).then_inc(stored, 16)
            sp.wait_ge(stored, 16 * ST)

        @block.gpsimd
        def _(pool):
            nc.gpsimd.memset(ident[:], 0.0).then_inc(consts_ready, 1)
            nc.gpsimd.memset(mask[:], 0.0).then_inc(consts_ready, 1)
            nc.gpsimd.memset(eps[:], EPS).then_inc(consts_ready, 1)
            pool.wait_ge(consts_ready, 3)
            nc.gpsimd.affine_select(out=ident[:], in_=ident[:], compare_op=ALU.not_equal, fill=1.0, base=0,
                                    pattern=[[-1, P]], channel_multiplier=1).then_inc(consts_ready, 1)
            nc.gpsimd.affine_select(out=mask[:], in_=mask[:], compare_op=ALU.is_ge, fill=MASKED, base=-1,
                                    pattern=[[1, 2 * P]], channel_multiplier=-1).then_inc(consts_ready, 1)
            pool.wait_ge(consts_ready, 5)
            nc.gpsimd.affine_select(out=mask[:], in_=mask[:], compare_op=ALU.is_ge, fill=MASKED, base=P,
                                    pattern=[[-1, 2 * P]], channel_multiplier=1).then_inc(consts_ready, 1)
            pool.wait_ge(un_ready, ST)
            nc.gpsimd.memset(kz_hi[:].bitcast(F32), 0.0).then_inc(kz_zero, 1)
            nc.gpsimd.memset(kz_lo[:].bitcast(F32), 0.0).then_inc(kz_zero, 1)
            nc.gpsimd.memset(stat[:, 127:128], 0.0).then_inc(mix_ready, 1)
            nc.gpsimd.memset(stat[:, 125:126], 0.0).then_inc(ix_done, 1)

            def gate_mix(c):
                pool.wait_ge(pv_read, 4 * c + 4)
                pool.wait_ge(gate_ready, c + 2)
                nc.gpsimd.tensor_tensor(mix[:, ds(2 * c, 2), :], mix[:, ds(2 * c, 2), :], gate[:], ALU.mult)\
                    .then_inc(mix_ready, 1)

            with pool.Fori(0, CHUNKS - 1) as c:
                gate_mix(c)
            gate_mix(CHUNKS - 1)

            pool.wait_ge(mix_ready, CHUNKS + 1)
            pool.wait_ge(mix_lo, CHUNKS)
            pool.dma_start(gain_post[:], norm_post[0:1, :].to_broadcast([P, D])).then_inc(post_landed, 16)
            pool.dma_start(gain_pre[:], norm_pre[1:2, :].to_broadcast([P, D])).then_inc(pre2_landed, 16)
            for st in range(ST):
                if st:
                    pool.wait_ge(h_ready, st)
                pool.dma_start(x_again[:], x[st * P:(st + 1) * P, :]).then_inc(again_landed, 16)

            def lru_product(j):
                pool.wait_ge(i_done, j + 1)
                nc.gpsimd.tensor_tensor(ig[:], ig[:], xc[:], ALU.mult).then_inc(ix_done, 1)

            with pool.Fori(0, CHUNKS - 1) as j:
                lru_product(j)
            lru_product(CHUNKS - 1)
            pool.wait_ge(lmix_ready, CHUNKS)
            pool.dma_start(gain_post[:], norm_post[1:2, :].to_broadcast([P, D])).then_inc(post_landed, 16)

        @block.scalar
        def _(act):
            def split_hi(s, u, landed_at, used):
                act.wait_ge(raw_landed[s], landed_at)
                if used is not None:
                    act.wait_ge(weights_used, used)
                nc.scalar.activation(w_hi[:, s, :], raw[:, s, :], ACT.Copy).then_inc(hi_done, 1)

            def split(u):
                split_hi(slot(u), u, landed(u), u - depth(u) + 1 if u >= depth(u) else None)

            def norm_turned(m):
                st = m % ST
                for j in range(4):
                    g = 4 * m + j
                    act.wait_ge(u_turned, g + 1)
                    nc.scalar.activation(u_hi[:, 4 * j:4 * j + 4, st * P:(st + 1) * P],
                                         bank[4 + j][:].rearrange("p (k s) -> p k s", k=4), ACT.Copy)\
                        .then_inc(u_hi_done, 1)

            act.wait_ge(consts_ready, 6)
            for st in range(ST):
                act.wait_ge(x_landed[st], 16)
                if st:
                    act.wait_ge(sq_done, st)
                nc.scalar.activation(square[:], h[:, st, :], ACT.Square, accum_out=stat[:, 2 * st:2 * st + 1])\
                    .then_inc(sq_done, 1)
                act.wait_ge(sq_done, st + 1)
                nc.scalar.activation(stat[:, 2 * st + 1:2 * st + 2], stat[:, 2 * st:2 * st + 1], ACT.Sqrt,
                                     bias=eps[:, 0:1], scale=1.0 / D).then_inc(root_done, 1)
                if st:
                    norm_turned(st - 1)
                if st >= 1:
                    split(st - 1)
            norm_turned(ST - 1)

            for p in range(8):
                if p + 3 < 12:
                    split(p + 3)
                if p == 3:
                    act.wait_ge(soft_step, 1)
                    nc.scalar.activation(soft[:, 1, :], soft[:, 0, :], ACT.Exp).then_inc(soft_exp, 1)
                    act.wait_ge(weights_used, U_K + 4)
                    for t in range(2):
                        for half in range(2):
                            nc.scalar.activation(kc[64 * half:64 * half + 64, 2 * t + 1, :],
                                                 bank[t][64:128, :], ACT.Copy).then_inc(k_kept, 1)

            def kz_build(c, group):
                act.wait_ge(k_kept, 8)
                act.wait_ge(kz_zero, 2)
                nc.scalar.activation(kz_hi[0:64, 0, :], kc[0:64, group, :], ACT.Copy).then_inc(kz_hi_done, 1)
                nc.scalar.activation(kz_hi[64:128, 1, :], kc[64:128, group, :], ACT.Copy).then_inc(kz_hi_done, 1)

            def v_build(c, group):
                act.wait_ge(v_kept, 4)
                for half in range(2):
                    nc.scalar.activation(v_hi[:, :, 64 * half:64 * half + 64],
                                         vc[:, :, ds(group * HEAD, HEAD)], ACT.Copy).then_inc(v_hi_done, 1)

            def q_kept(c):
                for t in range(2):
                    if t == 0:
                        act.wait_ge(q_proj, c + 1)
                    else:
                        act.wait_ge(weights_used, U_Q + 4 + 8 * c)
                    nc.scalar.activation(q_hi[:, t, :], bank[t][:], ACT.Copy, scale=HEAD ** -0.5)\
                        .then_inc(q_hi_done, 1)

            kz_build(0, 0)
            v_build(0, 0)
            for p in range(4):
                split(U_Q + p + 3)
            q_kept(0)

            def exps(c, b):
                e = 4 * c + b
                w = P if b == 0 else 2 * P
                act.wait_ge(shift_done, e + 1)
                for hd in range(4):
                    nc.scalar.activation(probs[:, b % 2, hd, 0:w], probs[:, b % 2, hd, 0:w], ACT.Exp,
                                         bias=shift[:, b % 2, hd:hd + 1],
                                         accum_out=row_sum[:, b % 2, hd:hd + 1]).then_inc(exp_done, 1)
                act.wait_ge(sink_shift_done, e + 1)
                nc.scalar.activation(sink_exp[:, b % 2, :], sink_shift[:, b % 2, :], ACT.Exp).then_inc(exp_done, 1)

            def att_slot(c, s):
                for step in ATT_STEPS.get(s, ()):
                    if step[0] == "S":
                        exps(c, step[1])
                    elif step[0] == "T":
                        _, b, k = step
                        act.wait_ge(p_turned, t_index(c, b, k) + 1)
                        if b:
                            act.wait_ge(pv_done, 4 * c + b)
                        nc.scalar.activation(pt_hi[:, k, :], bank[6][:], ACT.Copy).then_inc(pt_hi_done, 1)

            def att_body(c, last):
                for s in range(8 if last else 16):
                    att_slot(c, s)
                    if s % 2 == 0 and not last:
                        p = s // 2
                        u = U_ATT + 8 * c + p + 3
                        split_hi((p + 3) % DEPTH, u,
                                 16 * (2 * c + (U_ATT + p + 3) // DEPTH + 1), u - DEPTH + 1)
                    elif s % 2 == 0:
                        split(U_ATT + 8 * c + s // 2 + 3)
                    if s == 8 or (last and s == 7):
                        act.wait_ge(mix_ready, c + 1)
                        for t in range(2):
                            if t == 0:
                                act.wait_ge(gate_proj, c + 1)
                            else:
                                act.wait_ge(weights_used, U_ATT + 4 + 8 * c)
                            nc.scalar.activation(gate[:, t, :], bank[2 + t][:], ACT.Tanh, scale=0.5)\
                                .then_inc(gate_tanh, 1)
                if not last:
                    act.wait_ge(scores_done, 4 * c + 4)
                    kz_build(c + 1, (c + 1) // 2)
                    q_kept(c + 1)
                    act.wait_ge(pv_done, 4 * c + 4)
                    v_build(c + 1, (c + 1) // 2)

            with act.Fori(0, CHUNKS - 1) as c:
                att_body(c, False)
            att_body(CHUNKS - 1, True)

            def mix_split(base, w, ready):
                act.wait_ge(mix_ready if base == 0 else lmix_ready, ready)
                nc.scalar.activation(u_hi[:, 2 * w:2 * w + 2, :], mix[:, 2 * w:2 * w + 2, :], ACT.Copy)\
                    .then_inc(mix_hi, 1)

            def squares(layer, st, n, count):
                y = h if layer == 0 else y2
                act.wait_ge(o_copied, count)
                nc.scalar.activation(square[:, 512 * st:512 * st + 512], y[:, st, ds(512 * n, 512)], ACT.Square,
                                     accum_out=stat[:, ds(8 + 4 * st + n, 1)]).then_inc(o_squared, 1)

            def out_phase(layer, u0, extra):
                for p in range(8):
                    extra(p)
                    if p < 6:
                        mix_split(layer, p + 2, p + 2 + (2 if layer == 0 else 1))
                    split(u0 + p + 3)
                b0 = 16 * layer
                with act.Fori(1, 3) as n:
                    for p in range(8):
                        u = u0 + 8 * n + p + 3
                        s = (u0 + p + 3) % DEPTH
                        split_hi(s, u, 32 * n + landed(u0 + 8 + p + 3) - 32, u - DEPTH + 1)
                        if p < 4:
                            squares(layer, p, n - 1, b0 + 4 * (n - 1) + p + 1)
                        if p == 6:
                            act.wait_ge(o_squared, b0 + 4 * n)
                for half in range(2):
                    for p in range(8):
                        u = u0 + 24 + 8 * half + p + 3
                        if u < (U_LRU + 2 if layer == 0 else UNITS):
                            split(u)
                        if half == 0 and p < 4:
                            squares(layer, p, 2, b0 + 8 + p + 1)
                        if half == 0 and p == 6:
                            act.wait_ge(o_squared, b0 + 12)
                        if half == 1 and p in (1, 2):
                            squares(layer, p - 1, 3, b0 + 12 + p)
                        if half == 1 and p in (3, 5):
                            finish(layer, (p - 3) // 2)
                squares(layer, 2, 3, b0 + 15)
                squares(layer, 3, 3, b0 + 16)
                finish(layer, 2)
                finish(layer, 3)

            def finish(layer, st):
                act.wait_ge(sum_done, ST * layer + st + 1)
                f = 60 + 8 * (ST * layer + st)
                nc.scalar.activation(stat[:, f + 1:f + 2], stat[:, f:f + 1], ACT.Sqrt, bias=eps[:, 0:1],
                                     scale=1.0 / D).then_inc(root_done, 1)
                if layer == 0:
                    act.wait_ge(h_ready, st + 1)
                    nc.scalar.activation(un[:, st % 2, :], h[:, st, :], ACT.Square,
                                         accum_out=stat[:, f + 2:f + 3]).then_inc(sq_done, 1)
                    act.wait_ge(sq_done, ST + st + 1)
                    nc.scalar.activation(stat[:, f + 3:f + 4], stat[:, f + 2:f + 3], ACT.Sqrt, bias=eps[:, 0:1],
                                         scale=1.0 / D).then_inc(root_done, 1)
                    norm_turned(ST + st)

            def att_tail(p):
                for s in (8 + 2 * p, 9 + 2 * p):
                    att_slot(CHUNKS - 1, s)

            act.wait_ge(weights_used, U_O1)
            mix_split(0, 0, 2)
            mix_split(0, 1, 3)
            out_phase(0, U_O1, att_tail)

            for p in range(4):
                split(U_LRU + p + 2)

            def lru_body(j, last):
                def next_split(p):
                    if last:
                        split(U_LRU + 4 + 9 * j + p + 2)
                        return
                    u = U_LRU + 4 + 9 * j + p + 2
                    s = (4 + p + 2) % LRU_DEPTH
                    k0 = landed(U_LRU + 4 + p + 2)
                    per = landed(U_LRU + 13 + p + 2) - k0
                    split_hi(s, u, k0 + per * j, u - LRU_DEPTH + 1)

                def column(v, t):
                    return vec[:, ds(v + 2 * j + t, 1)]

                act.wait_ge(vec_ready, 1)
                act.wait_ge(ix_done, j + 1)
                for t in range(2):
                    if t == 0:
                        act.wait_ge(xb_proj, j + 1)
                    else:
                        act.wait_ge(weights_used, U_LRU + 4 + 9 * j)
                    nc.scalar.activation(xc[:, t, :], bank[t][:], ACT.Identity, bias=column(CONV_B, t),
                                         scale=column(CONV_W + 3 * KT, t)).then_inc(conv_begun, 1)
                next_split(0)
                act.wait_ge(conv_tap, 6 * j + 6)
                nc.scalar.activation(xc_hi[:], xc[:], ACT.Copy).then_inc(xc_hi_done, 1)
                for p in (1, 2, 3):
                    next_split(p)
                silu = lgate_last if last else lgate
                for t in range(2):
                    if t == 0 and not last:
                        act.wait_ge(lgate_proj, j + 1)
                    else:
                        act.wait_ge(weights_used, U_LRU + 8 + 9 * j)
                    nc.scalar.activation(silu[:, t, :], bank[2 + t][:], ACT.Tanh, scale=0.5)\
                        .then_inc(lgate_tanh, 1)
                next_split(4)
                for t in range(2):
                    act.wait_ge(ri_proj, 3 * j + t + 1)
                    nc.scalar.activation(rg[:, t, :], bank[4 + t][:], ACT.Sigmoid, bias=column(B_A, t))\
                        .then_inc(r_done, 1)
                for t in range(2):
                    if t == 0:
                        act.wait_ge(ri_proj, 3 * j + 3)
                    else:
                        act.wait_ge(weights_used, U_LRU + 9 + 9 * j)
                    ins = nc.scalar.activation(ig[:, t, :], bank[6 + t][:], ACT.Sigmoid, bias=column(B_X, t))
                ins.then_inc(i_done, 1)
                act.wait_ge(r_done, 2 * j + 2)
                for t in range(2):
                    nc.scalar.activation(rg[:, t, :], rg[:, t, :], ACT.Tanh, scale=sp4[:, ds(2 * j + t, 1)])\
                        .then_inc(t_done, 1)
                if not last:
                    next_split(5)
                act.wait_ge(t_done, 2 * j + 2)
                nc.scalar.activation(bt[:], rg[:], ACT.Sqrt, scale=4.0).then_inc(root_t_done, 1)
                if not last:
                    for p in (6, 7, 8):
                        next_split(p)

            with act.Fori(0, CHUNKS - 1) as j:
                lru_body(j, False)
            lru_body(CHUNKS - 1, True)
            mix_split(1, 0, 1)
            mix_split(1, 1, 2)
            split(U_O2 + 2)
            out_phase(1, U_O2, lambda p: None)

        @block.vector
        def _(dve):
            def split_lo(s, u):
                dve.wait_ge(hi_done, u + 1)
                nc.vector.tensor_tensor(w_lo[:, s, :], raw[:, s, :], w_hi[:, s, :].bitcast(F32), ALU.subtract)\
                    .then_inc(lo_done, 1)

            def split(u):
                split_lo(slot(u), u)

            def norm_turned(m):
                st = m % ST
                for j in range(4):
                    g = 4 * m + j
                    at = u_lo[:, 4 * j:4 * j + 4, st * P:(st + 1) * P]
                    dve.wait_ge(u_hi_done, g + 1)
                    nc.vector.tensor_tensor(at, bank[4 + j][:].rearrange("p (k s) -> p k s", k=4),
                                            u_hi[:, 4 * j:4 * j + 4, st * P:(st + 1) * P].bitcast(F32),
                                            ALU.subtract).then_inc(u_lo_done, 1)

            def scaled(dst, src, column, gain, n):
                rstd = stat[:, 40 + n:41 + n]
                nc.vector.reciprocal(rstd, stat[:, column:column + 1]).then_inc(rstd_done, 1)
                dve.wait_ge(rstd_done, n)
                return nc.vector.scalar_tensor_tensor(out=dst, in0=src, scalar=rstd, in1=gain,
                                                      op0=ALU.mult, op1=ALU.mult)

            for st in range(ST):
                dve.wait_ge(root_done, st + 1)
                if st == 0:
                    dve.wait_ge(pre_landed, 16)
                if st >= 2:
                    dve.wait_ge(u_turned, 4 * (st - 1))
                scaled(un[:, st % 2, :], h[:, st, :], 2 * st + 1, gain_pre[:], st + 1).then_inc(un_ready, 1)
                if st >= 1:
                    norm_turned(st - 1)
                    split(st - 1)
            dve.wait_ge(vec_turned, 1)
            norm_turned(ST - 1)
            nc.vector.tensor_copy(vec[:], bank[0][:, 0:P]).then_inc(vec_ready, 1)
            dve.wait_ge(vec_ready, 1)
            lamv = vec[:, LAM:LAM + KT]
            nc.vector.scalar_tensor_tensor(out=soft[:, 0, :], in0=lamv, scalar=-1.0, in1=lamv,
                                           op0=ALU.mult, op1=ALU.min).then_inc(soft_step, 1)
            nc.vector.tensor_scalar(nsink[:], nsink[:], -1.0, None, ALU.mult).then_inc(soft_step, 1)

            def softplus():
                n = [2]

                def step(ins):
                    n[0] += 1
                    ins.then_inc(soft_step, 1)
                    dve.wait_ge(soft_step, n[0])
                dve.wait_ge(soft_exp, 1)
                z, den, s, s2, acc = (soft[:, i, :] for i in range(1, 6))
                step(nc.vector.tensor_scalar(den, z, 2.0, None, ALU.add))
                step(nc.vector.reciprocal(den, den))
                step(nc.vector.tensor_tensor(s, z, den, ALU.mult))
                step(nc.vector.tensor_tensor(s2, s, s, ALU.mult))
                step(nc.vector.tensor_scalar(acc, s2, 1.0 / 17, 1.0 / 15, ALU.mult, ALU.add))
                for odd in (13, 11, 9, 7, 5, 3, 1):
                    step(nc.vector.tensor_tensor(acc, acc, s2, ALU.mult))
                    step(nc.vector.tensor_scalar(acc, acc, 1.0 / odd, None, ALU.add))
                step(nc.vector.tensor_tensor(acc, acc, s, ALU.mult))
                step(nc.vector.tensor_scalar(z, lamv, -1.0, 0.0, ALU.mult, ALU.max))
                step(nc.vector.scalar_tensor_tensor(out=acc, in0=acc, scalar=2.0, in1=z, op0=ALU.mult, op1=ALU.add))
                step(nc.vector.tensor_scalar(sp4[:], acc, 4.0, None, ALU.mult))

            for p in range(8):
                if p + 3 < 12:
                    split(p + 3)
                if p == 3:
                    dve.wait_ge(weights_used, U_K + 4)
                    dve.wait_ge(k_kept, 4)
                    for t in range(2):
                        for half in range(2):
                            nc.vector.tensor_copy(kc[64 * half:64 * half + 64, 2 * t, :], bank[t][0:64, :])\
                                .then_inc(k_kept, 1)
                    softplus()
            for b in range(NB):
                if b < NB - 1:
                    dve.wait_ge(v_proj, b + 1)
                else:
                    dve.wait_ge(weights_used, U_V + 4)
                nc.vector.tensor_copy(vc[:, b, :], bank[4 + b][:, 0:KV_W]).then_inc(v_kept, 1)

            def kz_build(c, group):
                dve.wait_ge(kz_hi_done, 2 * c + 2)
                for half in range(2):
                    rows = slice(64 * half, 64 * half + 64)
                    nc.vector.tensor_tensor(kz_lo[rows, half, :], kc[rows, group, :],
                                            kz_hi[rows, half, :].bitcast(F32), ALU.subtract).then_inc(kz_lo_done, 1)

            def v_build(c, group):
                dve.wait_ge(v_hi_done, 2 * c + 2)
                for half in range(2):
                    at = slice(64 * half, 64 * half + 64)
                    nc.vector.tensor_tensor(v_lo[:, :, at], vc[:, :, ds(group * HEAD, HEAD)],
                                            v_hi[:, :, at].bitcast(F32), ALU.subtract).then_inc(v_lo_done, 1)

            def q_kept(c):
                for t in range(2):
                    dve.wait_ge(q_hi_done, 2 * c + t + 1)
                    nc.vector.scalar_tensor_tensor(out=q_lo[:, t, :], in0=bank[t][:], scalar=HEAD ** -0.5,
                                                   in1=q_hi[:, t, :].bitcast(F32), op0=ALU.mult,
                                                   op1=ALU.subtract).then_inc(q_lo_done, 1)

            kz_build(0, 0)
            v_build(0, 0)
            for p in range(4):
                split(U_Q + p + 3)
            q_kept(0)
            nc.vector.memset(stat[:, 126:127], 0.0).then_inc(gate_ready, 1)

            def mask_max(c, b):
                e = 4 * c + b
                w = P if b == 0 else 2 * P
                buf = b % 2
                dve.wait_ge(scores_done, e + 1)
                for t in range(2):
                    nc.vector.tensor_tensor(
                        probs[:, buf, 2 * t:2 * t + 2, 0:w], bank[4 + t][:, 0:2 * w].rearrange("p (h k) -> p h k", h=2),
                        mask[:, 2 * P - w:2 * P].unsqueeze(1).to_broadcast([P, 2, w]), ALU.add)\
                        .then_inc(scores_masked, 1)
                dve.wait_ge(scores_masked, 2 * e + 2)
                nc.vector.tensor_reduce(row_max[:, buf, :], probs[:, buf, :, 0:w], AX_X, ALU.max)\
                    .then_inc(max_done, 1)
                dve.wait_ge(max_done, e + 1)
                nc.vector.scalar_tensor_tensor(out=shift[:, buf, :], in0=row_max[:, buf, :], scalar=-1.0,
                                               in1=nsink[:, ds(4 * c, 4)], op0=ALU.mult, op1=ALU.min)\
                    .then_inc(shift_done, 1)
                dve.wait_ge(shift_done, e + 1)
                nc.vector.tensor_tensor(sink_shift[:, buf, :], shift[:, buf, :], nsink[:, ds(4 * c, 4)],
                                        ALU.subtract).then_inc(sink_shift_done, 1)

            def normalise(c, b):
                e = 4 * c + b
                w = P if b == 0 else 2 * P
                buf = b % 2
                dve.wait_ge(exp_done, 5 * e + 5)
                nc.vector.tensor_tensor(denom[:, buf, :], row_sum[:, buf, :], sink_exp[:, buf, :], ALU.add)\
                    .then_inc(denom_done, 1)
                dve.wait_ge(denom_done, e + 1)
                nc.vector.reciprocal(denom[:, buf, :], denom[:, buf, :]).then_inc(recip_done, 1)
                dve.wait_ge(recip_done, e + 1)
                nc.vector.tensor_tensor(probs[:, buf, :, 0:w], probs[:, buf, :, 0:w],
                                        denom[:, buf, :].unsqueeze(2).to_broadcast([P, 4, w]), ALU.mult)\
                    .then_inc(probs_ready, 1)

            def att_slot(c, s):
                for step in ATT_STEPS.get(s - 1, ()):
                    if step[0] == "S":
                        normalise(c, step[1])
                for step in ATT_STEPS.get(s, ()):
                    if step[0] == "S":
                        mask_max(c, step[1])
                    elif step[0] == "T":
                        _, b, k = step
                        dve.wait_ge(pt_hi_done, t_index(c, b, k) + 1)
                        nc.vector.tensor_tensor(pt_lo[:, k, :], bank[6][:], pt_hi[:, k, :].bitcast(F32),
                                                ALU.subtract).then_inc(pt_lo_done, 1)
                    else:
                        b = step[1]
                        dve.wait_ge(pv_done, 4 * c + b + 1)
                        for half in range(2):
                            rows = slice(64 * half, 64 * half + 64)
                            src = bank[7][rows, :].rearrange("p (t e q) -> p t e q", t=2, e=2)[:, :, half, :]
                            ins = nc.vector.tensor_scalar(mix[rows, ds(2 * c, 2), b * P:(b + 1) * P], src, 0.5,
                                                          None, ALU.mult)
                        ins.then_inc(pv_read, 1)

            def att_body(c, last):
                for s in range(8 if last else 16):
                    att_slot(c, s)
                    if s % 2 == 0 and not last:
                        p = s // 2
                        split_lo((p + 3) % DEPTH, U_ATT + 8 * c + p + 3)
                    elif s % 2 == 0:
                        split(U_ATT + 8 * c + s // 2 + 3)
                    if s == 8 or (last and s == 7):
                        for t in range(2):
                            dve.wait_ge(gate_tanh, 2 * c + t + 1)
                            ins = nc.vector.scalar_tensor_tensor(out=gate[:, t, :], in0=gate[:, t, :], scalar=1.0,
                                                                 in1=bank[2 + t][:], op0=ALU.add, op1=ALU.mult)
                        ins.then_inc(gate_ready, 1)
                if not last:
                    kz_build(c + 1, (c + 1) // 2)
                    q_kept(c + 1)
                    v_build(c + 1, (c + 1) // 2)

            with dve.Fori(0, CHUNKS - 1) as c:
                att_body(c, False)
            att_body(CHUNKS - 1, True)

            def mix_split(layer, w):
                dve.wait_ge(mix_hi, CHUNKS * layer + w + 1)
                nc.vector.tensor_tensor(u_lo[:, 2 * w:2 * w + 2, :], mix[:, 2 * w:2 * w + 2, :],
                                        u_hi[:, 2 * w:2 * w + 2, :].bitcast(F32), ALU.subtract).then_inc(mix_lo, 1)

            def copies(layer, st, n):
                y = h if layer == 0 else y2
                u0 = U_O2 if layer else U_O1
                last = st == ST - 1
                if isinstance(n, int) and n == 3:
                    if st % 2:
                        dve.wait_ge(weights_used, u0 + 24 + 8 * (st // 2) + 8)
                    else:
                        dve.wait_ge(o_done, 11 * layer + 10 + st // 2)
                elif last:
                    dve.wait_ge(weights_used, u0 + 8 * n + 8)
                else:
                    dve.wait_ge(o_done, 11 * layer + 3 * n + st + 1)
                nc.vector.tensor_copy(y[:, st, ds(512 * n, 512)], bank[st][:]).then_inc(o_copied, 1)

            def out_phase(layer, u0, extra):
                for p in range(8):
                    extra(p)
                    if p < 6:
                        mix_split(layer, p + 2)
                    split(u0 + p + 3)
                with dve.Fori(1, 3) as n:
                    for p in range(8):
                        if p == 0:
                            for st in range(ST):
                                copies(layer, st, n - 1)
                        split_lo((u0 + p + 3) % DEPTH, u0 + 8 * n + p + 3)
                for half in range(2):
                    for p in range(8):
                        u = u0 + 24 + 8 * half + p + 3
                        if half == 0 and p == 0:
                            for st in range(ST):
                                copies(layer, st, 2)
                        if half == 1 and p in (0, 1):
                            copies(layer, p, 3)
                        if u < (U_LRU + 2 if layer == 0 else UNITS):
                            split(u)
                        if half == 1 and p in (3, 5):
                            finish(layer, (p - 3) // 2)
                copies(layer, 2, 3)
                copies(layer, 3, 3)
                finish(layer, 2)
                finish(layer, 3)

            def finish(layer, st):
                y = h if layer == 0 else y2
                dve.wait_ge(o_squared, 16 * layer + 13 + st)
                f = 60 + 8 * (ST * layer + st)
                nc.vector.tensor_reduce(stat[:, f:f + 1], stat[:, 8 + 4 * st:12 + 4 * st], AX_X, ALU.add)\
                    .then_inc(sum_done, 1)
                dve.wait_ge(root_done, 5 + 2 * st if layer == 0 else 13 + st)
                if st == 0:
                    dve.wait_ge(post_landed, 16 * (layer + 1))
                n = 5 + 2 * st if layer == 0 else 13 + st
                scaled(y[:, st, :], y[:, st, :], f + 1, gain_post[:], n).then_inc(scaled_done, 1)
                dve.wait_ge(scaled_done, ST * layer + st + 1)
                if layer == 0:
                    dve.wait_ge(again_landed, 16 * (st + 1))
                    nc.vector.tensor_tensor(h[:, st, :], h[:, st, :], x_again[:], ALU.add).then_inc(h_ready, 1)
                    dve.wait_ge(root_done, 6 + 2 * st)
                    if st == 0:
                        dve.wait_ge(pre2_landed, 16)
                    if st >= 2:
                        dve.wait_ge(u_turned, 4 * (ST + st - 1))
                    scaled(un[:, st % 2, :], h[:, st, :], f + 3, gain_pre[:], 6 + 2 * st).then_inc(un_ready, 1)
                    norm_turned(ST + st)
                else:
                    nc.vector.tensor_tensor(h[:, st, :], h[:, st, :], y2[:, st, :], ALU.add).then_inc(h_ready, 1)

            def att_tail(p):
                for s in (8 + 2 * p, 9 + 2 * p):
                    att_slot(CHUNKS - 1, s)

            mix_split(0, 0)
            mix_split(0, 1)
            out_phase(0, U_O1, att_tail)

            for p in range(4):
                split(U_LRU + p + 2)

            def lru_body(j, last):
                def next_split(p):
                    split_lo((4 + p + 2) % LRU_DEPTH if not last else slot(U_LRU + 4 + 9 * j + p + 2),
                             U_LRU + 4 + 9 * j + p + 2)

                dve.wait_ge(conv_begun, 2 * j + 2)
                for back in (1, 2, 3):
                    if back > 1:
                        dve.wait_ge(conv_tap, 6 * j + 2 * back - 2)
                    for t in range(2):
                        nc.vector.scalar_tensor_tensor(
                            out=xc[:, t, back:SEQ], in0=bank[t][:, 0:SEQ - back],
                            scalar=vec[:, ds(CONV_W + (3 - back) * KT + 2 * j + t, 1)], in1=xc[:, t, back:SEQ],
                            op0=ALU.mult, op1=ALU.add).then_inc(conv_tap, 1)
                next_split(0)
                dve.wait_ge(xc_hi_done, j + 1)
                nc.vector.tensor_tensor(xc_lo[:], xc[:], xc_hi[:].bitcast(F32), ALU.subtract).then_inc(xc_lo_done, 1)
                for p in (1, 2, 3):
                    next_split(p)
                silu = lgate_last if last else lgate
                for t in range(2):
                    dve.wait_ge(lgate_tanh, 2 * j + t + 1)
                    nc.vector.scalar_tensor_tensor(out=silu[:, t, :], in0=silu[:, t, :], scalar=1.0,
                                                   in1=bank[2 + t][:], op0=ALU.add, op1=ALU.mult)\
                        .then_inc(lgate_ready, 1)
                next_split(4)
                dve.wait_ge(t_done, 2 * j + 2)
                nc.vector.tensor_scalar(decay[:], rg[:], 1.0, None, ALU.add).then_inc(one_plus_t, 1)
                if not last:
                    next_split(5)
                dve.wait_ge(one_plus_t, j + 1)
                for t in range(2):
                    nc.vector.reciprocal(decay[:, t, :], decay[:, t, :]).then_inc(q_recip, 1)
                    if t == 0 and not last:
                        next_split(6)
                dve.wait_ge(q_recip, 2 * j + 2)
                dve.wait_ge(root_t_done, j + 1)
                nc.vector.tensor_tensor(bt[:], bt[:], decay[:], ALU.mult).then_inc(b_step, 1)
                dve.wait_ge(b_step, 2 * j + 1)
                nc.vector.tensor_scalar(decay[:], decay[:], 2.0, -1.0, ALU.mult, ALU.add).then_inc(a_done, 1)
                if not last:
                    next_split(7)
                dve.wait_ge(ix_done, j + 2)
                nc.vector.tensor_tensor(bt[:], bt[:], ig[:], ALU.mult).then_inc(b_step, 1)
                dve.wait_ge(a_done, j + 1)
                dve.wait_ge(b_step, 2 * j + 2)
                for t in range(2):
                    nc.vector.tensor_tensor_scan(rg[:, t, :], decay[:, t, :], bt[:, t, :], 0.0, ALU.mult, ALU.add)\
                        .then_inc(scan_done, 1)
                if not last:
                    next_split(8)
                dve.wait_ge(scan_done, 2 * j + 2)
                dve.wait_ge(lgate_ready, 2 * j + 2)
                nc.vector.scalar_tensor_tensor(out=mix[:, ds(2 * j, 2), :], in0=rg[:], scalar=0.5, in1=silu[:],
                                               op0=ALU.mult, op1=ALU.mult).then_inc(lmix_ready, 1)

            with dve.Fori(0, CHUNKS - 1) as j:
                lru_body(j, False)
            lru_body(CHUNKS - 1, True)
            mix_split(1, 0)
            mix_split(1, 1)
            split(U_O2 + 2)
            out_phase(1, U_O2, lambda p: None)

        @block.tensor
        def _(pe):
            def weights(s):
                return (w_hi[:, s, :].rearrange("p (k n) -> p k n", n=256),
                        w_lo[:, s, :].rearrange("p (k n) -> p k n", n=256))

            def three(out_ap, lhs_hi, lhs_lo, rhs_hi, rhs_lo, start, stop):
                pe.matmul(out_ap, lhs_hi, rhs_hi, start=start, stop=False)
                pe.matmul(out_ap, lhs_hi, rhs_lo, start=False, stop=False)
                return pe.matmul(out_ap, lhs_lo, rhs_hi, start=False, stop=stop)

            def project(s, part, banks, tile):
                hi, lo = weights(s)
                for kk in range(4):
                    kt = 4 * part + kk
                    cols = slice(tile * P, (tile + 1) * P)
                    ins = three(bank[banks + tile][:], hi[:, kk, cols], lo[:, kk, cols], u_hi[:, kt, :],
                                u_lo[:, kt, :], kt == 0, kt == KT - 1)
                return ins

            def turn(m):
                pe.wait_ge(un_ready, m + 1)
                for j in range(4):
                    g = 4 * m + j
                    if g >= 4:
                        pe.wait_ge(u_lo_done, g - 3)
                    for k in range(4):
                        ins = pe.transpose(bank[4 + j][:, k * P:(k + 1) * P],
                                           un[:, m % 2, (4 * j + k) * P:(4 * j + k + 1) * P], ident[:])
                    ins.then_inc(u_turned, 1)

            pe.wait_ge(consts_ready, 6)
            pe.wait_ge(small_landed, 16 * 6)
            pe.transpose(bank[0][:, 0:P], vec_rows[:], ident[:]).then_inc(vec_turned, 1)
            for m in range(ST):
                turn(m)
            pe.wait_ge(u_lo_done, 4 * ST)
            pe.wait_ge(vec_ready, 1)
            for j in range(4):
                pe.wait_ge(lo_done, U_K + j + 1)
                for tile in range(2):
                    ins = project(slot(U_K + j), j, 0, tile)
                ins.then_inc(weights_used, 1)
            for j in range(4):
                pe.wait_ge(lo_done, U_V + j + 1)
                hi, lo = weights(slot(U_V + j))
                for st in range(ST):
                    cols = slice(st * P, (st + 1) * P)
                    for kk in range(4):
                        kt = 4 * j + kk
                        ins = three(bank[4 + st][:, 0:KV_W], u_hi[:, kt, cols], u_lo[:, kt, cols], hi[:, kk, :],
                                    lo[:, kk, :], kt == 0, kt == KT - 1)
                    if st == ST - 1:
                        ins.then_inc(weights_used, 1)
                    elif j == 3:
                        ins.then_inc(v_proj, 1)
            pe.wait_ge(k_kept, 8)
            for j in range(4):
                pe.wait_ge(lo_done, U_Q + j + 1)
                for tile in range(2):
                    ins = project(slot(U_Q + j), j, 0, tile)
                    if tile:
                        ins.then_inc(weights_used, 1)
                    elif j == 3:
                        ins.then_inc(q_proj, 1)

            def scores(c, b):
                w = P if b == 0 else 2 * P
                k0 = max(b - 1, 0) * P
                if b == 0:
                    pe.wait_ge(q_lo_done, 2 * c + 2)
                    pe.wait_ge(kz_lo_done, 2 * c + 2)
                else:
                    pe.wait_ge(scores_masked, 2 * (4 * c + b))
                for t in range(2):
                    q = slice(b * P, (b + 1) * P)
                    keys = slice(k0, k0 + w)
                    ins = three(bank[4 + t][:, 0:2 * w].rearrange("p (h k) -> p h k", h=2), q_hi[:, t, q],
                                q_lo[:, t, q], kz_hi[:, :, keys], kz_lo[:, :, keys], True, True)
                ins.then_inc(scores_done, 1)

            def turn_probs(c, b, k):
                if b == 0 or k == 0:
                    pe.wait_ge(probs_ready, 4 * c + b + 1)
                if b:
                    pe.wait_ge(pt_lo_done, t_index(c, b, k))
                at = 0 if b == 0 else k * P
                for hd in range(4):
                    ins = pe.transpose(bank[6][:, hd * P:(hd + 1) * P], probs[:, b % 2, hd, at:at + P], ident[:])
                ins.then_inc(p_turned, 1)

            def weigh_values(c, b):
                if b == 0:
                    pe.wait_ge(v_lo_done, 2 * c + 2)
                    pe.wait_ge(mix_ready, c + 1)
                else:
                    pe.wait_ge(pv_read, 4 * c + b)
                pe.wait_ge(pt_lo_done, t_index(c, b, 1) + 1)
                for k in ((1,) if b == 0 else (0, 1)):
                    kb = b - 1 + k
                    ins = three(bank[7][:], v_hi[:, kb, :], v_lo[:, kb, :], pt_hi[:, k, :], pt_lo[:, k, :],
                                b == 0 or k == 0, k == 1)
                ins.then_inc(pv_done, 1)

            def att_slot(c, s):
                for step in ATT_STEPS.get(s, ()):
                    if step[0] == "S":
                        scores(c, step[1])
                    elif step[0] == "T":
                        turn_probs(c, step[1], step[2])
                    else:
                        weigh_values(c, step[1])

            def att_body(c, last):
                for p in range(4 if last else 8):
                    pe.wait_ge(lo_done, U_ATT + 8 * c + p + 1)
                    gates = p < 4
                    if p == 0:
                        pe.wait_ge(gate_ready, c + 1)
                    if p == 4:
                        pe.wait_ge(q_lo_done, 2 * c + 2)
                    for tile in range(2):
                        ins = project(p % DEPTH, p % 4, 2 if gates else 0, tile)
                        if tile:
                            ins.then_inc(weights_used, 1)
                        elif p % 4 == 3:
                            ins.then_inc(gate_proj if gates else q_proj, 1)
                        att_slot(c, 2 * p + tile)

            with pe.Fori(0, CHUNKS - 1) as c:
                att_body(c, False)
            att_body(CHUNKS - 1, True)

            def out_unit(s, p, tiles, done):
                hi = w_hi[:, s, :].rearrange("p (k n) -> p k n", n=512)
                lo = w_lo[:, s, :].rearrange("p (k n) -> p k n", n=512)
                for st in tiles:
                    cols = slice(st * P, (st + 1) * P)
                    for kk in range(2):
                        kt = 2 * p + kk
                        ins = three(bank[st][:], u_hi[:, kt, cols], u_lo[:, kt, cols], hi[:, kk, :], lo[:, kk, :],
                                    kt == 0, kt == KT - 1)
                    if st == tiles[-1]:
                        ins.then_inc(weights_used, 1)
                    elif p == 7:
                        ins.then_inc(o_done, 1)
                    done(st)

            def out_phase(layer, u0):
                b0 = 16 * layer
                for p in range(8):
                    pe.wait_ge(lo_done, u0 + p + 1)
                    pe.wait_ge(mix_lo, CHUNKS * layer + p + 1)

                    def attention(st, p=p):
                        if layer == 0 and st % 2 and p < 4:
                            att_slot(CHUNKS - 1, 8 + 2 * p + st // 2)
                    out_unit((u0 + p) % DEPTH, p, range(ST), attention)
                with pe.Fori(1, 3) as n:
                    for p in range(8):
                        pe.wait_ge(lo_done, u0 + 8 * n + p + 1)

                        if p == 0:
                            pe.wait_ge(o_copied, b0 + 4 * n - 3)

                        def copied(st, p=p):
                            if p == 0 and st < ST - 1:
                                pe.wait_ge(o_copied, b0 + 4 * n - 3 + st + 1)
                        out_unit((u0 + p) % DEPTH, p, range(ST), copied)
                for half in range(2):
                    for p in range(8):
                        pe.wait_ge(lo_done, u0 + 24 + 8 * half + p + 1)
                        if p == 0:
                            pe.wait_ge(o_copied, b0 + 10 + 2 * half)
                        out_unit((u0 + p) % DEPTH, p, range(2 * half, 2 * half + 2), lambda st: None)
                        if layer == 0 and half == 1 and p in (6, 7):
                            turn(ST + p - 6)
                if layer == 0:
                    turn(ST + 2)
                    turn(ST + 3)

            pe.wait_ge(q_lo_done, 2 * CHUNKS)
            pe.wait_ge(gate_ready, CHUNKS + 1)
            out_phase(0, U_O1)

            pe.wait_ge(u_lo_done, 8 * ST)
            pe.wait_ge(o_copied, 16)
            for j in range(4):
                pe.wait_ge(lo_done, U_LRU + j + 1)
                for tile in range(2):
                    ins = project(slot(U_LRU + j), j, 0, tile)
                    if tile:
                        ins.then_inc(weights_used, 1)
                    elif j == 3:
                        ins.then_inc(xb_proj, 1)

            def lru_body(j, last):
                for p in range(5 if last else 9):
                    s = (4 + p) % LRU_DEPTH
                    pe.wait_ge(lo_done, U_LRU + 4 + 9 * j + p + 1)
                    if p == 4:
                        pe.wait_ge(xc_lo_done, j + 1)
                        hi, lo = weights(s)
                        for g in range(2):
                            for tile in range(2):
                                cols = slice(tile * P, (tile + 1) * P)
                                for kk in range(2):
                                    ins = three(bank[4 + 2 * g + tile][:], hi[:, 2 * g + kk, cols],
                                                lo[:, 2 * g + kk, cols], xc_hi[:, kk, :], xc_lo[:, kk, :],
                                                kk == 0, kk == 1)
                                if g and tile:
                                    ins.then_inc(weights_used, 1)
                                else:
                                    ins.then_inc(ri_proj, 1)
                        continue
                    gates = p < 4
                    if p == 5:
                        pe.wait_ge(conv_tap, 6 * j + 6)
                    for tile in range(2):
                        ins = project(s, p if gates else p - 5, 2 if gates else 0, tile)
                        if tile:
                            ins.then_inc(weights_used, 1)
                        elif p in (3, 8):
                            ins.then_inc(lgate_proj if gates else xb_proj, 1)
                pe.wait_ge(lgate_ready, 2 * j + 2)

            with pe.Fori(0, CHUNKS - 1) as j:
                lru_body(j, False)
            lru_body(CHUNKS - 1, True)
            pe.wait_ge(conv_tap, 6 * CHUNKS)
            out_phase(1, U_O2)


def program(nc, a, out):
    rows = lambda ap, spec, **k: ap.rearrange(spec, **k)
    build(
        nc,
        rows(a["x"], "b s d -> (b s) d"), a["norm_pre"], a["norm_post"],
        rows(a["attn_w_in"], "a k n -> (a k) n"), rows(a["attn_w_out"], "a k n -> (a k) n"), a["attn_sinks"],
        rows(a["lru_w_in"], "a k n -> (a k) n"),
        rows(a["lru_conv_w"], "a c (t p) -> (a c t) p", p=P), rows(a["lru_conv_b"], "a (t p) -> (a t) p", p=P),
        rows(a["lru_w_a"], "a g i o -> (a g i) o"), rows(a["lru_b_a"], "a g (t p) -> (a g t) p", p=P),
        rows(a["lru_w_x"], "a g i o -> (a g i) o"), rows(a["lru_b_x"], "a g (t p) -> (a g t) p", p=P),
        rows(a["lru_lambda"], "a (t p) -> (a t) p", p=P),
        rows(a["lru_w_out"], "a k n -> (a k) n"),
        rows(out, "b s d -> (b s) d"),
    )


INPUTS = ["x", "norm_pre", "norm_post", "attn_w_in", "attn_w_out", "attn_sinks", "lru_w_in", "lru_conv_w",
          "lru_conv_b", "lru_w_a", "lru_b_a", "lru_w_x", "lru_b_x", "lru_lambda", "lru_w_out"]


def kernel(**inputs):
    import numpy as np
    import concourse.bacc as bacc
    from concourse.bass_utils import run_bass_kernel_spmd

    nc = bacc.Bacc("TRN2", target_bir_lowering=False, num_devices=1)
    arrays, args = {}, {}
    for name in INPUTS:
        a = np.ascontiguousarray(inputs[name])
        arrays[f"in_{name}"] = a
        args[name] = nc.dram_tensor(f"in_{name}", a.shape, mybir.dt.from_np(a.dtype), kind="ExternalInput").ap()
    out = nc.dram_tensor("out", (1, SEQ, D), F32, kind="ExternalOutput").ap()
    program(nc, args, out)
    return run_bass_kernel_spmd(nc, [arrays], core_ids=[0]).results[0]["out"]
```

```python
from contextlib import ExitStack

import concourse.bass as bass
from concourse import mybir

F32 = mybir.dt.float32
F32R = mybir.dt.float32r
ALU = mybir.AluOpType
ACT = mybir.ActivationFunctionType
AX_X = mybir.AxisListType.X
ds = bass.ds

P = 128
SEQ = 512
D = 2048
KT = D // P
ST = SEQ // P
HEAD = 64
HEADS = D // HEAD
KV_HEADS = HEADS // 8
KV_W = KV_HEADS * HEAD
CHUNKS = D // 256
NB = SEQ // P
EPS = 1e-6
MASKED = -1e30
CONV = 4
LRU_BW = 256

DEPTH = 4
LRU_DEPTH = 3
U_V, U_K, U_Q = 0, 4, 8
U_ATT = 12
U_O1 = U_ATT + 8 * CHUNKS - 4
U_LRU = U_O1 + 40
U_O2 = U_LRU + 9 * CHUNKS
UNITS = U_O2 + 40

ATT_STEPS = {1: [("S", 0)], 3: [("S", 1)], 5: [("T", 0, 1)], 6: [("V", 0), ("S", 2)], 7: [("T", 1, 0)],
             8: [("T", 1, 1)], 9: [("V", 1), ("S", 3)], 10: [("T", 2, 0)], 11: [("T", 2, 1)], 12: [("V", 2)],
             13: [("T", 3, 0)], 14: [("T", 3, 1)], 15: [("V", 3)]}

ROOTS = ([("x", st) for st in range(4)]
         + [("A", 0), ("B", 0), ("A", 1), ("B", 1), ("A", 2), ("A", 3), ("B", 2), ("B", 3)]
         + [("C", st) for st in range(4)])


def t_index(c, b, k):
    return 7 * c + (0 if b == 0 else 2 * b - 1 + k)


def root_count(kind, st):
    return ROOTS.index((kind, st)) + 1


def depth(u):
    return DEPTH if u < U_LRU or u > U_O2 + 2 else LRU_DEPTH


def slot(u):
    return (u - U_LRU) % LRU_DEPTH if U_LRU <= u < U_O2 else u % DEPTH


def landed(u):
    n = 0
    for v in range(u + 1):
        if slot(v) == slot(u):
            n += 16
            if U_LRU <= v < U_O2 and (v - U_LRU) % 9 == 8:
                n += 16
    return n


def build(nc, x, norm_pre, norm_post, w_in, w_out, sinks, l_in, conv_w, conv_b, w_a, b_a, w_x, b_x,
          lam, l_out, out):
    ctx = ExitStack()
    with ctx:
        base = (nc.sbuf_base + 63) // 64 * 64
        cursor = [base]

        def place(name, shape, dt, at=None):
            size = 4
            for n in shape[1:]:
                size *= n
            if at is None:
                at = cursor[0]
                cursor[0] += (size + 31) // 32 * 32
            return nc.alloc_sbuf_tensor_at(name, shape, dt, offset=at)

        def sem(name):
            return ctx.enter_context(nc.semaphore(name))

        u_hi = place("u_hi", [P, KT, SEQ], F32R)
        u_lo = place("u_lo", [P, KT, SEQ], F32R)
        y_at = cursor[0]
        mix = place("mix", [P, KT, SEQ], F32)
        h_at = cursor[0]
        h = place("h", [P, ST, D], F32)
        raw_at = cursor[0]
        raw = place("raw", [P, DEPTH, 1024], F32)
        w_hi = place("w_hi", [P, DEPTH, 1024], F32R)
        w_lo = place("w_lo", [P, DEPTH, 1024], F32R)
        ident = place("ident", [P, P], F32)
        vec = place("vec", [P, P], F32)
        mask = place("mask", [P, 2 * P], F32)
        nsink = place("nsink", [P, HEADS], F32)
        eps = place("eps", [P, 1], F32)
        stat = place("stat", [P, 128], F32)
        soft = place("soft", [P, 6, KT], F32)
        sp4 = place("sp4", [P, KT], F32)
        row_max = place("row_max", [P, 2, 4], F32)
        shift = place("shift", [P, 2, 4], F32)
        sink_shift = place("sink_shift", [P, 2, 4], F32)
        row_sum = place("row_sum", [P, 2, 4], F32)
        sink_exp = place("sink_exp", [P, 2, 4], F32)
        denom = place("denom", [P, 2, 4], F32)
        t_at = (cursor[0] + 63) // 64 * 64
        assert t_at + 7 * 4096 <= nc.sbuf_usable_end, (t_at, nc.sbuf_usable_end)
        K = 1024
        gain_pre = place("gain_pre", [P, D], F32, y_at)
        un = place("un", [P, 2, D], F32, y_at + 8 * K)
        square = place("square", [P, D], F32, t_at)
        gain_post = place("gain_post", [P, D], F32, t_at + 8 * K)
        x_again = [place(f"x_again{i}", [P, D], F32, t_at + 16 * K * i) for i in range(2)]
        dump = place("dump", [P, SEQ], F32, t_at + 24 * K)
        vec_rows = place("vec_rows", [P, P], F32, t_at + 26 * K)
        gain_row = place("gain_row", [1, D], F32, t_at + 16 * K)
        ones_row = place("ones_row", [1, P], F32, t_at + 27 * K)
        y2 = place("y2", [P, ST, D], F32, y_at)
        kc = place("kc", [P, KV_HEADS, SEQ], F32, h_at)
        probs = place("probs", [P, 2, 4, 2 * P], F32, h_at + 8 * K)
        kz_hi = place("kz_hi", [P, 2, SEQ], F32R, h_at + 16 * K)
        kz_lo = place("kz_lo", [P, 2, SEQ], F32R, h_at + 20 * K)
        pt_hi = place("pt_hi", [P, 2, SEQ], F32R, h_at + 24 * K)
        pt_lo = place("pt_lo", [P, 2, SEQ], F32R, h_at + 28 * K)
        q_hi = place("q_hi", [P, 2, SEQ], F32R, t_at)
        q_lo = place("q_lo", [P, 2, SEQ], F32R, t_at + 4 * K)
        gate = place("gate", [P, 2, SEQ], F32, t_at + 8 * K)
        v_hi = place("v_hi", [P, NB, P], F32R, t_at + 12 * K)
        v_lo = place("v_lo", [P, NB, P], F32R, t_at + 14 * K)
        vc = place("vc", [P, NB, KV_W], F32, t_at + 16 * K)
        xc = place("xc", [P, 2, SEQ], F32, t_at)
        xc_hi = place("xc_hi", [P, 2, SEQ], F32R, t_at + 4 * K)
        xc_lo = place("xc_lo", [P, 2, SEQ], F32R, t_at + 8 * K)
        rg = place("rg", [P, 2, SEQ], F32, t_at + 12 * K)
        bt = place("bt", [P, 2, SEQ], F32, t_at + 16 * K)
        ig = place("ig", [P, 2, SEQ], F32, t_at + 20 * K)
        decay = place("decay", [P, 2, SEQ], F32, t_at + 24 * K)
        lgate = place("lgate", [P, 2, SEQ], F32, raw_at + 3 * 4 * K)
        lgate_last = place("lgate_last", [P, 2, SEQ], F32, base + 14 * 2 * K)
        bank = [ctx.enter_context(nc.psum_tensor(f"bank{i}", [P, 512], F32)) for i in range(8)]

        x_landed = [sem(f"x_landed{i}") for i in range(ST)]
        small_landed = sem("small_landed")
        row_landed = sem("row_landed")
        gain_spread = sem("gain_spread")
        gain_kept = sem("gain_kept")
        pre2_landed = sem("pre2_landed")
        post_landed = sem("post_landed")
        again_landed = [sem(f"again_landed{i}") for i in range(2)]
        raw_landed = [sem(f"raw_landed{i}") for i in range(DEPTH)]
        hi_done = sem("hi_done")
        lo_done = sem("lo_done")
        weights_used = sem("weights_used")
        consts_ready = sem("consts_ready")
        kz_zero = sem("kz_zero")
        vec_turned = sem("vec_turned")
        vec_ready = sem("vec_ready")
        soft_step = sem("soft_step")
        soft_exp = sem("soft_exp")
        sq_done = sem("sq_done")
        root_done = sem("root_done")
        sum_done = sem("sum_done")
        rstd_done = sem("rstd_done")
        scaled_done = sem("scaled_done")
        hg_done = sem("hg_done")
        h_ready = sem("h_ready")
        un_ready = sem("un_ready")
        u_turned = sem("u_turned")
        u_hi_done = sem("u_hi_done")
        u_lo_done = sem("u_lo_done")
        v_proj = sem("v_proj")
        k_kept = sem("k_kept")
        v_kept = sem("v_kept")
        q_proj = sem("q_proj")
        q_hi_done = sem("q_hi_done")
        q_lo_done = sem("q_lo_done")
        gate_proj = sem("gate_proj")
        gate_tanh = sem("gate_tanh")
        gate_ready = sem("gate_ready")
        kz_hi_done = sem("kz_hi_done")
        kz_lo_done = sem("kz_lo_done")
        v_hi_done = sem("v_hi_done")
        v_lo_done = sem("v_lo_done")
        scores_done = sem("scores_done")
        scores_masked = sem("scores_masked")
        max_done = sem("max_done")
        shift_done = sem("shift_done")
        sink_shift_done = sem("sink_shift_done")
        exp_done = sem("exp_done")
        denom_done = sem("denom_done")
        recip_done = sem("recip_done")
        probs_ready = sem("probs_ready")
        p_turned = sem("p_turned")
        pt_hi_done = sem("pt_hi_done")
        pt_lo_done = sem("pt_lo_done")
        pv_done = sem("pv_done")
        pv_read = sem("pv_read")
        mix_ready = sem("mix_ready")
        mix_hi = sem("mix_hi")
        mix_lo = sem("mix_lo")
        o_done = sem("o_done")
        o_copied = sem("o_copied")
        o_squared = sem("o_squared")
        xb_proj = sem("xb_proj")
        conv_begun = sem("conv_begun")
        conv_tap = sem("conv_tap")
        xc_hi_done = sem("xc_hi_done")
        xc_lo_done = sem("xc_lo_done")
        lgate_proj = sem("lgate_proj")
        lgate_tanh = sem("lgate_tanh")
        lgate_ready = sem("lgate_ready")
        ri_proj = sem("ri_proj")
        r_done = sem("r_done")
        i_done = sem("i_done")
        t_done = sem("t_done")
        root_t_done = sem("root_t_done")
        one_plus_t = sem("one_plus_t")
        q_recip = sem("q_recip")
        b_step = sem("b_step")
        a_done = sem("a_done")
        ix_done = sem("ix_done")
        scan_done = sem("scan_done")
        lmix_ready = sem("lmix_ready")
        stored = sem("stored")

        LAM, B_A, B_X, CONV_B, CONV_W = 0, 16, 32, 48, 64

        def w_unit(w, row0, kts, col0, cols):
            return w[ds(row0, kts * P), ds(col0, cols)].rearrange("(k p) n -> p k n", p=P)

        def bcast(ap, shape):
            return ap.to_broadcast(shape)

        block = ctx.enter_context(nc.Block())

        @block.sync
        def _(sp):
            def load(s, u, free_after, src, parts=1):
                if free_after is not None:
                    sp.wait_ge(lo_done, free_after)
                dst = raw[:, s, :].rearrange("p (k n) -> p k n", n=src[0].shape[2])
                at = 0
                for part in src:
                    k = part.shape[1]
                    sp.dma_start(dst[:, at:at + k, :], part).then_inc(raw_landed[s], 16)
                    at += k

            def free(u):
                return u - depth(u) + 1 if u >= depth(u) else None

            def load_x(st):
                sp.dma_start(h[:, st, :], x[st * P:(st + 1) * P, :]).then_inc(x_landed[st], 16)

            def load_kv(u0, j, col0):
                load(slot(u0 + j), u0 + j, free(u0 + j), [w_unit(w_in, j * 512, 4, col0, 256)])

            sp.dma_start(gain_row[:], norm_pre[0:1, :]).then_inc(row_landed, 16)
            load_x(0)
            load_kv(U_V, 0, D + KV_W)
            load_kv(U_V, 1, D + KV_W)
            load_x(1)
            load_kv(U_V, 2, D + KV_W)
            load_kv(U_V, 3, D + KV_W)
            load_x(2)
            load_x(3)
            sp.dma_start(nsink[:], sinks.to_broadcast([P, HEADS])).then_inc(small_landed, 16)
            rows = [(lam, LAM, 1), (b_a, B_A, 1), (b_x, B_X, 1), (conv_b, CONV_B, 1), (conv_w, CONV_W, CONV)]
            for v, r0, n in rows:
                sp.dma_start(vec_rows[r0:r0 + n * KT, :], v).then_inc(small_landed, 16)
            for j in range(4):
                load_kv(U_K, j, D)
            for j in range(4):
                load_kv(U_Q, j, 0)

            def att_units(i, last):
                g0 = D + 2 * KV_W
                for p in range(4 if last else 8):
                    u = U_ATT + 8 * i + p
                    src = w_unit(w_in, (p % 4) * 512, 4, g0 + 256 * i if p < 4 else 256 * i + 256, 256)
                    load(p % DEPTH, u, u - DEPTH + 1, [src])

            with sp.Fori(0, CHUNKS - 1) as i:
                att_units(i, False)
            att_units(CHUNKS - 1, True)

            def out_units(w, u0):
                def chunk(n, u0n, frees):
                    for p in range(8):
                        if isinstance(n, int) and n == 0 and p == 3 and u0 == U_O2:
                            sp.wait_ge(lmix_ready, CHUNKS - 1)
                        load(p % DEPTH, u0n + p, frees(p), [w_unit(w, p * 256, 2, 512 * n, 512)])
                chunk(0, u0, lambda p: free(u0 + p))
                with sp.Fori(1, 3) as n:
                    chunk(n, u0 + 8 * n, lambda p: u0 + 8 * n + p - DEPTH + 1)
                for half in range(2):
                    chunk(3, u0 + 24 + 8 * half, lambda p: free(u0 + 24 + 8 * half + p))

            out_units(w_out, U_O1)

            def lru_units(j, last):
                for p in range(5 if last else 9):
                    u = U_LRU + 4 + 9 * j + p
                    if p < 4:
                        src = [w_unit(l_in, p * 512, 4, D + 256 * j, 256)]
                    elif p == 4:
                        src = [w_unit(w_a, LRU_BW * j, 2, 0, 256), w_unit(w_x, LRU_BW * j, 2, 0, 256)]
                    else:
                        src = [w_unit(l_in, (p - 5) * 512, 4, 256 * j + 256, 256)]
                    load((4 + p) % LRU_DEPTH, u, u - LRU_DEPTH + 1, src)

            for j in range(4):
                load(slot(U_LRU + j), U_LRU + j, free(U_LRU + j), [w_unit(l_in, j * 512, 4, 0, 256)])
            with sp.Fori(0, CHUNKS - 1) as j:
                lru_units(j, False)
            lru_units(CHUNKS - 1, True)
            out_units(l_out, U_O2)

            for st in range(ST):
                for half in range(2):
                    sp.wait_ge(h_ready, 4 * (ST + st) + 2 * half + 2)
                    cols = slice(half * D // 2, (half + 1) * D // 2)
                    sp.dma_start(out[st * P:(st + 1) * P, cols], h[:, st, cols]).then_inc(stored, 16)
            sp.wait_ge(stored, 32 * ST)

        @block.gpsimd
        def _(pool):
            nc.gpsimd.memset(ones_row[:], 1.0).then_inc(consts_ready, 1)
            nc.gpsimd.memset(ident[:], 0.0).then_inc(consts_ready, 1)
            nc.gpsimd.memset(mask[:], 0.0).then_inc(consts_ready, 1)
            nc.gpsimd.memset(eps[:], EPS).then_inc(consts_ready, 1)
            pool.wait_ge(consts_ready, 4)
            nc.gpsimd.affine_select(out=ident[:], in_=ident[:], compare_op=ALU.not_equal, fill=1.0, base=0,
                                    pattern=[[-1, P]], channel_multiplier=1).then_inc(consts_ready, 1)
            nc.gpsimd.affine_select(out=mask[:], in_=mask[:], compare_op=ALU.is_ge, fill=MASKED, base=-1,
                                    pattern=[[1, 2 * P]], channel_multiplier=-1).then_inc(consts_ready, 1)
            pool.wait_ge(consts_ready, 6)
            nc.gpsimd.affine_select(out=mask[:], in_=mask[:], compare_op=ALU.is_ge, fill=MASKED, base=P,
                                    pattern=[[-1, 2 * P]], channel_multiplier=1).then_inc(consts_ready, 1)
            pool.wait_ge(un_ready, 4 * ST)
            nc.gpsimd.memset(kz_hi[:].bitcast(F32), 0.0).then_inc(kz_zero, 1)
            nc.gpsimd.memset(kz_lo[:].bitcast(F32), 0.0).then_inc(kz_zero, 1)
            nc.gpsimd.memset(stat[:, 127:128], 0.0).then_inc(mix_ready, 1)
            nc.gpsimd.memset(stat[:, 125:126], 0.0).then_inc(ix_done, 1)

            def gate_mix(c):
                pool.wait_ge(pv_read, 4 * c + 4)
                pool.wait_ge(gate_ready, c + 2)
                nc.gpsimd.tensor_tensor(mix[:, ds(2 * c, 2), :], mix[:, ds(2 * c, 2), :], gate[:], ALU.mult)\
                    .then_inc(mix_ready, 1)

            with pool.Fori(0, CHUNKS - 1) as c:
                gate_mix(c)
            gate_mix(CHUNKS - 1)

            pool.wait_ge(mix_ready, CHUNKS + 1)
            pool.dma_start(gain_post[:], norm_post[0:1, :].to_broadcast([P, D])).then_inc(post_landed, 16)
            for st in range(2):
                pool.dma_start(x_again[st][:], x[st * P:(st + 1) * P, :]).then_inc(again_landed[st], 16)
            pool.wait_ge(mix_lo, CHUNKS)
            pool.dma_start(gain_pre[:], norm_pre[1:2, :].to_broadcast([P, D])).then_inc(pre2_landed, 16)
            pool.wait_ge(pre2_landed, 16)
            for st in range(ST):
                if st >= 2:
                    pool.wait_ge(u_turned, 4 * (ST + st - 1))
                for j in range(4):
                    cols = slice(512 * j, 512 * j + 512)
                    pool.wait_ge(h_ready, 4 * st + j + 1)
                    nc.gpsimd.tensor_tensor(un[:, st % 2, cols], h[:, st, cols], gain_pre[:, cols], ALU.mult)\
                        .then_inc(hg_done, 1)
                if st < 2:
                    pool.dma_start(x_again[st][:], x[(st + 2) * P:(st + 3) * P, :]).then_inc(again_landed[st], 16)

            def lru_product(j):
                pool.wait_ge(i_done, j + 1)
                nc.gpsimd.tensor_tensor(ig[:], ig[:], xc[:], ALU.mult).then_inc(ix_done, 1)

            with pool.Fori(0, CHUNKS - 1) as j:
                lru_product(j)
            lru_product(CHUNKS - 1)
            pool.wait_ge(lmix_ready, CHUNKS)
            pool.dma_start(gain_post[:], norm_post[1:2, :].to_broadcast([P, D])).then_inc(post_landed, 16)

        @block.scalar
        def _(act):
            def split_hi(s, u, landed_at, used):
                act.wait_ge(raw_landed[s], landed_at)
                if used is not None:
                    act.wait_ge(weights_used, used)
                nc.scalar.activation(w_hi[:, s, :], raw[:, s, :], ACT.Copy).then_inc(hi_done, 1)

            def split(u):
                split_hi(slot(u), u, landed(u), u - depth(u) + 1 if u >= depth(u) else None)

            def norm_turned(m):
                st = m % ST
                for j in range(4):
                    g = 4 * m + j
                    act.wait_ge(u_turned, g + 1)
                    nc.scalar.activation(u_hi[:, 4 * j:4 * j + 4, st * P:(st + 1) * P],
                                         bank[4 + j][:].rearrange("p (k s) -> p k s", k=4), ACT.Copy)\
                        .then_inc(u_hi_done, 1)

            act.wait_ge(consts_ready, 7)
            for j in range(4):
                act.wait_ge(gain_spread, j + 1)
                nc.scalar.activation(gain_pre[:, 512 * j:512 * j + 512], bank[j][:], ACT.Copy)\
                    .then_inc(gain_kept, 1)
            for st in range(ST):
                act.wait_ge(x_landed[st], 16)
                nc.scalar.activation(square[:], h[:, st, :], ACT.Square, accum_out=stat[:, 2 * st:2 * st + 1])\
                    .then_inc(sq_done, 1)
                act.wait_ge(sq_done, st + 1)
                nc.scalar.activation(stat[:, 2 * st + 1:2 * st + 2], stat[:, 2 * st:2 * st + 1], ACT.Sqrt,
                                     bias=eps[:, 0:1], scale=1.0 / D).then_inc(root_done, 1)
                if st < 2:
                    split(U_V + 2 * st)
                    split(U_V + 2 * st + 1)
                if st:
                    norm_turned(st - 1)
            norm_turned(ST - 1)
            for j in range(7):
                split(U_K + j)
            act.wait_ge(weights_used, U_K + 4)
            for t in range(2):
                for half in range(2):
                    nc.scalar.activation(kc[64 * half:64 * half + 64, 2 * t + 1, :],
                                         bank[4 + t][64:128, :], ACT.Copy).then_inc(k_kept, 1)

            def kz_build(c, group):
                act.wait_ge(k_kept, 8)
                act.wait_ge(kz_zero, 2)
                nc.scalar.activation(kz_hi[0:64, 0, :], kc[0:64, group, :], ACT.Copy).then_inc(kz_hi_done, 1)
                nc.scalar.activation(kz_hi[64:128, 1, :], kc[64:128, group, :], ACT.Copy).then_inc(kz_hi_done, 1)

            def v_build(c, group):
                act.wait_ge(v_kept, 4)
                for half in range(2):
                    nc.scalar.activation(v_hi[:, :, 64 * half:64 * half + 64],
                                         vc[:, :, ds(group * HEAD, HEAD)], ACT.Copy).then_inc(v_hi_done, 1)

            def q_kept(c):
                for t in range(2):
                    if t == 0:
                        act.wait_ge(q_proj, c + 1)
                    else:
                        act.wait_ge(weights_used, U_Q + 4 + 8 * c)
                    nc.scalar.activation(q_hi[:, t, :], bank[t][:], ACT.Copy, scale=HEAD ** -0.5)\
                        .then_inc(q_hi_done, 1)

            kz_build(0, 0)
            v_build(0, 0)
            for p in range(4):
                split(U_Q + p + 3)
                if p == 1:
                    act.wait_ge(soft_step, 1)
                    nc.scalar.activation(soft[:, 1, :], soft[:, 0, :], ACT.Exp).then_inc(soft_exp, 1)
            q_kept(0)

            def exps(c, b):
                e = 4 * c + b
                w = P if b == 0 else 2 * P
                act.wait_ge(shift_done, e + 1)
                for hd in range(4):
                    nc.scalar.activation(probs[:, b % 2, hd, 0:w], probs[:, b % 2, hd, 0:w], ACT.Exp,
                                         bias=shift[:, b % 2, hd:hd + 1],
                                         accum_out=row_sum[:, b % 2, hd:hd + 1]).then_inc(exp_done, 1)
                act.wait_ge(sink_shift_done, e + 1)
                nc.scalar.activation(sink_exp[:, b % 2, :], sink_shift[:, b % 2, :], ACT.Exp).then_inc(exp_done, 1)

            def att_slot(c, s):
                for step in ATT_STEPS.get(s, ()):
                    if step[0] == "T":
                        _, b, k = step
                        act.wait_ge(p_turned, t_index(c, b, k) + 1)
                        if b:
                            act.wait_ge(pv_done, 4 * c + b)
                        nc.scalar.activation(pt_hi[:, k, :], bank[6][:], ACT.Copy).then_inc(pt_hi_done, 1)
                for step in ATT_STEPS.get(s - 1, ()):
                    if step[0] == "S":
                        exps(c, step[1])

            def mix_split(layer, w):
                act.wait_ge(lmix_ready if layer else mix_ready, w + (1 if layer else 2))
                act.wait_ge(weights_used, (U_O2 - 1 if layer else U_O1) - 3 + w // 2)
                nc.scalar.activation(u_hi[:, 2 * w:2 * w + 2, :], mix[:, 2 * w:2 * w + 2, :], ACT.Copy)\
                    .then_inc(mix_hi, 1)

            def att_body(c, last):
                for s in range(8 if last else 16):
                    att_slot(c, s)
                    if s % 2 == 0 and not last:
                        p = s // 2
                        u = U_ATT + 8 * c + p + 3
                        split_hi((p + 3) % DEPTH, u,
                                 16 * (2 * c + (U_ATT + p + 3) // DEPTH + 1), u - DEPTH + 1)
                    elif s % 2 == 0:
                        split(U_ATT + 8 * c + s // 2 + 3)
                    if last and s in (4, 5, 6):
                        mix_split(0, s - 4)
                    if s == 8 or (last and s == 7):
                        act.wait_ge(mix_ready, c + 1)
                        for t in range(2):
                            if t == 0:
                                act.wait_ge(gate_proj, c + 1)
                            else:
                                act.wait_ge(weights_used, U_ATT + 4 + 8 * c)
                            nc.scalar.activation(gate[:, t, :], bank[2 + t][:], ACT.Tanh, scale=0.5)\
                                .then_inc(gate_tanh, 1)
                if not last:
                    act.wait_ge(scores_done, 4 * c + 4)
                    kz_build(c + 1, (c + 1) // 2)
                    q_kept(c + 1)
                    act.wait_ge(pv_done, 4 * c + 4)
                    v_build(c + 1, (c + 1) // 2)

            with act.Fori(0, CHUNKS - 1) as c:
                att_body(c, False)
            att_body(CHUNKS - 1, True)

            def squares(layer, st, n):
                u0 = U_O2 if layer else U_O1
                if isinstance(n, int) and n == 3:
                    if st % 2:
                        act.wait_ge(weights_used, u0 + 24 + 8 * (st // 2) + 8)
                    else:
                        act.wait_ge(o_done, 11 * layer + 10 + st // 2)
                elif st == ST - 1:
                    act.wait_ge(weights_used, u0 + 8 * n + 8)
                else:
                    act.wait_ge(o_done, 11 * layer + 3 * n + st + 1)
                nc.scalar.activation(dump[:], bank[st][:], ACT.Square,
                                     accum_out=stat[:, ds(8 + 4 * st + n, 1)]).then_inc(o_squared, 1)
                act.wait_ge(o_squared, 16 * layer + 4 * n + st + 1)

            def root(kind, st):
                n = root_count(kind, st)
                act.wait_ge(sum_done, n - ST)
                nc.scalar.activation(stat[:, 80 + n:81 + n], stat[:, 60 + n:61 + n], ACT.Sqrt,
                                     bias=eps[:, 0:1], scale=1.0 / D).then_inc(root_done, 1)

            def residual_squares(st):
                for j in range(4):
                    act.wait_ge(h_ready, 4 * st + j + 1)
                    nc.scalar.activation(dump[:], h[:, st, 512 * j:512 * j + 512], ACT.Square,
                                         accum_out=stat[:, 100 + 4 * st + j:101 + 4 * st + j]).then_inc(sq_done, 1)
                    act.wait_ge(sq_done, ST + 4 * st + j + 1)

            def out_phase(layer, u0, extra):
                for p in range(8):
                    extra(p)
                    if p < 4:
                        mix_split(layer, p + 3)
                    if p == 5:
                        mix_split(layer, 7)
                    split(u0 + p + 3)
                with act.Fori(1, 3) as n:
                    for p in range(8):
                        if p == 0:
                            for st in range(ST):
                                squares(layer, st, n - 1)
                        u = u0 + 8 * n + p + 3
                        s = (u0 + p + 3) % DEPTH
                        split_hi(s, u, 32 * n + landed(u0 + 8 + p + 3) - 32, u - DEPTH + 1)
                for half in range(2):
                    for p in range(8):
                        u = u0 + 24 + 8 * half + p + 3
                        if half == 0 and p == 0:
                            for st in range(ST):
                                squares(layer, st, 2)
                        if half == 1 and p == 0:
                            squares(layer, 0, 3)
                            squares(layer, 1, 3)
                        if u < (U_LRU + 3 if layer == 0 else UNITS):
                            split(u)
                        if half == 1 and p in (0, 3):
                            st = p // 3
                            root("C" if layer else "A", st)
                            if layer == 0:
                                residual_squares(st)
                        if layer == 0 and half == 1 and p in (2, 5):
                            root("B", p // 5)
                            norm_turned(ST + p // 5)
                squares(layer, 2, 3)
                squares(layer, 3, 3)
                root("C" if layer else "A", 2)
                root("C" if layer else "A", 3)
                if layer == 0:
                    for st in (2, 3):
                        residual_squares(st)
                    for st in (2, 3):
                        root("B", st)
                        norm_turned(ST + st)

            def att_tail(p):
                for s in (8 + 2 * p, 9 + 2 * p):
                    att_slot(CHUNKS - 1, s)

            out_phase(0, U_O1, att_tail)

            for p in range(3):
                split(U_LRU + p + 3)

            def lru_body(j, last):
                def next_split(p):
                    if last:
                        split(U_LRU + 4 + 9 * j + p + 2)
                        return
                    u = U_LRU + 4 + 9 * j + p + 2
                    s = (4 + p + 2) % LRU_DEPTH
                    k0 = landed(U_LRU + 4 + p + 2)
                    per = landed(U_LRU + 13 + p + 2) - k0
                    split_hi(s, u, k0 + per * j, u - LRU_DEPTH + 1)

                def column(v, t):
                    return vec[:, ds(v + 2 * j + t, 1)]

                act.wait_ge(vec_ready, 1)
                act.wait_ge(ix_done, j + 1)
                for t in range(2):
                    if t == 0:
                        act.wait_ge(xb_proj, j + 1)
                    else:
                        act.wait_ge(weights_used, U_LRU + 4 + 9 * j)
                    nc.scalar.activation(xc[:, t, :], bank[t][:], ACT.Identity, bias=column(CONV_B, t),
                                         scale=column(CONV_W + 3 * KT, t)).then_inc(conv_begun, 1)
                next_split(0)
                act.wait_ge(conv_tap, 6 * j + 6)
                nc.scalar.activation(xc_hi[:], xc[:], ACT.Copy).then_inc(xc_hi_done, 1)
                for p in (1, 2, 3):
                    next_split(p)
                silu = lgate_last if last else lgate
                for t in range(2):
                    if t == 0 and not last:
                        act.wait_ge(lgate_proj, j + 1)
                    else:
                        act.wait_ge(weights_used, U_LRU + 8 + 9 * j)
                    nc.scalar.activation(silu[:, t, :], bank[2 + t][:], ACT.Tanh, scale=0.5)\
                        .then_inc(lgate_tanh, 1)
                next_split(4)
                if last:
                    for w in range(3):
                        mix_split(1, w)
                for t in range(2):
                    act.wait_ge(ri_proj, 3 * j + t + 1)
                    nc.scalar.activation(rg[:, t, :], bank[4 + t][:], ACT.Sigmoid, bias=column(B_A, t))\
                        .then_inc(r_done, 1)
                for t in range(2):
                    if t == 0:
                        act.wait_ge(ri_proj, 3 * j + 3)
                    else:
                        act.wait_ge(weights_used, U_LRU + 9 + 9 * j)
                    ins = nc.scalar.activation(ig[:, t, :], bank[6 + t][:], ACT.Sigmoid, bias=column(B_X, t))
                ins.then_inc(i_done, 1)
                act.wait_ge(r_done, 2 * j + 2)
                for t in range(2):
                    nc.scalar.activation(rg[:, t, :], rg[:, t, :], ACT.Tanh, scale=sp4[:, ds(2 * j + t, 1)])\
                        .then_inc(t_done, 1)
                if not last:
                    next_split(5)
                act.wait_ge(t_done, 2 * j + 2)
                nc.scalar.activation(bt[:], rg[:], ACT.Sqrt, scale=4.0).then_inc(root_t_done, 1)
                if not last:
                    for p in (6, 7, 8):
                        next_split(p)

            with act.Fori(0, CHUNKS - 1) as j:
                lru_body(j, False)
            lru_body(CHUNKS - 1, True)
            split(U_O2 + 2)
            out_phase(1, U_O2, lambda p: None)

        @block.vector
        def _(dve):
            def split_lo(s, u):
                dve.wait_ge(hi_done, u + 1)
                nc.vector.tensor_tensor(w_lo[:, s, :], raw[:, s, :], w_hi[:, s, :].bitcast(F32), ALU.subtract)\
                    .then_inc(lo_done, 1)

            def split(u):
                split_lo(slot(u), u)

            def norm_turned(m):
                st = m % ST
                for j in range(4):
                    g = 4 * m + j
                    at = u_lo[:, 4 * j:4 * j + 4, st * P:(st + 1) * P]
                    dve.wait_ge(u_hi_done, g + 1)
                    nc.vector.tensor_tensor(at, bank[4 + j][:].rearrange("p (k s) -> p k s", k=4),
                                            u_hi[:, 4 * j:4 * j + 4, st * P:(st + 1) * P].bitcast(F32),
                                            ALU.subtract).then_inc(u_lo_done, 1)

            def reciprocal_root(kind, st, column):
                n = root_count(kind, st)
                rstd = stat[:, 40 + n:41 + n]
                dve.wait_ge(root_done, n)
                nc.vector.reciprocal(rstd, stat[:, column:column + 1]).then_inc(rstd_done, 1)
                dve.wait_ge(rstd_done, n)
                return rstd

            def norm_x(st):
                if st == 0:
                    dve.wait_ge(gain_kept, 4)
                rstd = reciprocal_root("x", st, 2 * st + 1)
                if st >= 2:
                    dve.wait_ge(u_turned, 4 * (st - 1))
                for j in range(4):
                    cols = slice(512 * j, 512 * j + 512)
                    nc.vector.scalar_tensor_tensor(out=un[:, st % 2, cols], in0=h[:, st, cols], scalar=rstd,
                                                   in1=gain_pre[:, cols], op0=ALU.mult, op1=ALU.mult)\
                        .then_inc(un_ready, 1)

            split(0)
            norm_x(0)
            split(1)
            norm_turned(0)
            split(2)
            norm_x(1)
            split(3)
            norm_turned(1)
            norm_x(2)

            def keep_values(b):
                if b < NB - 1:
                    dve.wait_ge(v_proj, b + 1)
                else:
                    dve.wait_ge(weights_used, U_V + 4)
                nc.vector.tensor_copy(vc[:, b, :], bank[b][:, 0:KV_W]).then_inc(v_kept, 1)

            norm_turned(2)
            norm_x(3)
            norm_turned(3)
            for b in range(NB - 1):
                keep_values(b)
            split(U_K)
            keep_values(NB - 1)
            for j in range(1, 7):
                split(U_K + j)
            dve.wait_ge(weights_used, U_K + 4)
            dve.wait_ge(k_kept, 4)
            for t in range(2):
                for half in range(2):
                    nc.vector.tensor_copy(kc[64 * half:64 * half + 64, 2 * t, :], bank[4 + t][0:64, :])\
                        .then_inc(k_kept, 1)
            lamv = vec[:, LAM:LAM + KT]

            def softplus():
                n = [2]

                def step(ins):
                    n[0] += 1
                    ins.then_inc(soft_step, 1)
                    dve.wait_ge(soft_step, n[0])
                dve.wait_ge(soft_exp, 1)
                z, den, s, s2, acc = (soft[:, i, :] for i in range(1, 6))
                step(nc.vector.tensor_scalar(den, z, 2.0, None, ALU.add))
                step(nc.vector.reciprocal(den, den))
                step(nc.vector.tensor_tensor(s, z, den, ALU.mult))
                step(nc.vector.tensor_tensor(s2, s, s, ALU.mult))
                step(nc.vector.tensor_scalar(acc, s2, 1.0 / 17, 1.0 / 15, ALU.mult, ALU.add))
                for odd in (13, 11, 9, 7, 5, 3, 1):
                    step(nc.vector.tensor_tensor(acc, acc, s2, ALU.mult))
                    step(nc.vector.tensor_scalar(acc, acc, 1.0 / odd, None, ALU.add))
                step(nc.vector.tensor_tensor(acc, acc, s, ALU.mult))
                step(nc.vector.tensor_scalar(z, lamv, -1.0, 0.0, ALU.mult, ALU.max))
                step(nc.vector.scalar_tensor_tensor(out=acc, in0=acc, scalar=2.0, in1=z, op0=ALU.mult, op1=ALU.add))
                step(nc.vector.tensor_scalar(sp4[:], acc, 4.0, None, ALU.mult))

            def kz_build(c, group):
                dve.wait_ge(kz_hi_done, 2 * c + 2)
                for half in range(2):
                    rows = slice(64 * half, 64 * half + 64)
                    nc.vector.tensor_tensor(kz_lo[rows, half, :], kc[rows, group, :],
                                            kz_hi[rows, half, :].bitcast(F32), ALU.subtract).then_inc(kz_lo_done, 1)

            def v_build(c, group):
                dve.wait_ge(v_hi_done, 2 * c + 2)
                for half in range(2):
                    at = slice(64 * half, 64 * half + 64)
                    nc.vector.tensor_tensor(v_lo[:, :, at], vc[:, :, ds(group * HEAD, HEAD)],
                                            v_hi[:, :, at].bitcast(F32), ALU.subtract).then_inc(v_lo_done, 1)

            def q_kept(c):
                for t in range(2):
                    dve.wait_ge(q_hi_done, 2 * c + t + 1)
                    nc.vector.scalar_tensor_tensor(out=q_lo[:, t, :], in0=bank[t][:], scalar=HEAD ** -0.5,
                                                   in1=q_hi[:, t, :].bitcast(F32), op0=ALU.mult,
                                                   op1=ALU.subtract).then_inc(q_lo_done, 1)

            kz_build(0, 0)
            v_build(0, 0)
            split(U_Q + 3)
            dve.wait_ge(vec_turned, 1)
            nc.vector.tensor_copy(vec[:], bank[6][:, 0:P]).then_inc(vec_ready, 1)
            dve.wait_ge(vec_ready, 1)
            nc.vector.scalar_tensor_tensor(out=soft[:, 0, :], in0=lamv, scalar=-1.0, in1=lamv,
                                           op0=ALU.mult, op1=ALU.min).then_inc(soft_step, 1)
            nc.vector.tensor_scalar(nsink[:], nsink[:], -1.0, None, ALU.mult).then_inc(soft_step, 1)
            split(U_Q + 4)
            softplus()
            split(U_Q + 5)
            split(U_Q + 6)
            q_kept(0)
            nc.vector.memset(stat[:, 126:127], 0.0).then_inc(gate_ready, 1)

            def mask_max(c, b):
                e = 4 * c + b
                w = P if b == 0 else 2 * P
                buf = b % 2
                dve.wait_ge(scores_done, e + 1)
                for t in range(2):
                    nc.vector.tensor_tensor(
                        probs[:, buf, 2 * t:2 * t + 2, 0:w], bank[4 + t][:, 0:2 * w].rearrange("p (h k) -> p h k", h=2),
                        mask[:, 2 * P - w:2 * P].unsqueeze(1).to_broadcast([P, 2, w]), ALU.add)\
                        .then_inc(scores_masked, 1)
                dve.wait_ge(scores_masked, 2 * e + 2)
                nc.vector.tensor_reduce(row_max[:, buf, :], probs[:, buf, :, 0:w], AX_X, ALU.max)\
                    .then_inc(max_done, 1)
                dve.wait_ge(max_done, e + 1)
                nc.vector.scalar_tensor_tensor(out=shift[:, buf, :], in0=row_max[:, buf, :], scalar=-1.0,
                                               in1=nsink[:, ds(4 * c, 4)], op0=ALU.mult, op1=ALU.min)\
                    .then_inc(shift_done, 1)
                dve.wait_ge(shift_done, e + 1)
                nc.vector.tensor_tensor(sink_shift[:, buf, :], shift[:, buf, :], nsink[:, ds(4 * c, 4)],
                                        ALU.subtract).then_inc(sink_shift_done, 1)

            def normalise(c, b):
                e = 4 * c + b
                w = P if b == 0 else 2 * P
                buf = b % 2
                dve.wait_ge(exp_done, 5 * e + 5)
                nc.vector.tensor_tensor(denom[:, buf, :], row_sum[:, buf, :], sink_exp[:, buf, :], ALU.add)\
                    .then_inc(denom_done, 1)
                dve.wait_ge(denom_done, e + 1)
                nc.vector.reciprocal(denom[:, buf, :], denom[:, buf, :]).then_inc(recip_done, 1)
                dve.wait_ge(recip_done, e + 1)
                nc.vector.tensor_tensor(probs[:, buf, :, 0:w], probs[:, buf, :, 0:w],
                                        denom[:, buf, :].unsqueeze(2).to_broadcast([P, 4, w]), ALU.mult)\
                    .then_inc(probs_ready, 1)

            def att_slot(c, s):
                for step in ATT_STEPS.get(s, ()):
                    if step[0] == "T":
                        _, b, k = step
                        dve.wait_ge(pt_hi_done, t_index(c, b, k) + 1)
                        nc.vector.tensor_tensor(pt_lo[:, k, :], bank[6][:], pt_hi[:, k, :].bitcast(F32),
                                                ALU.subtract).then_inc(pt_lo_done, 1)
                    elif step[0] == "V":
                        b = step[1]
                        dve.wait_ge(pv_done, 4 * c + b + 1)
                        for half in range(2):
                            rows = slice(64 * half, 64 * half + 64)
                            src = bank[7][rows, :].rearrange("p (t e q) -> p t e q", t=2, e=2)[:, :, half, :]
                            ins = nc.vector.tensor_scalar(mix[rows, ds(2 * c, 2), b * P:(b + 1) * P], src, 0.5,
                                                          None, ALU.mult)
                        ins.then_inc(pv_read, 1)
                for step in ATT_STEPS.get(s - 2, ()):
                    if step[0] == "S":
                        normalise(c, step[1])
                for step in ATT_STEPS.get(s, ()):
                    if step[0] == "S":
                        mask_max(c, step[1])

            def mix_split(layer, w):
                dve.wait_ge(mix_hi, CHUNKS * layer + w + 1)
                nc.vector.tensor_tensor(u_lo[:, 2 * w:2 * w + 2, :], mix[:, 2 * w:2 * w + 2, :],
                                        u_hi[:, 2 * w:2 * w + 2, :].bitcast(F32), ALU.subtract).then_inc(mix_lo, 1)

            def att_body(c, last):
                for s in range(8 if last else 16):
                    att_slot(c, s)
                    if s % 2 == 0 and not last:
                        p = s // 2
                        split_lo((p + 3) % DEPTH, U_ATT + 8 * c + p + 3)
                    elif s % 2 == 0:
                        split(U_ATT + 8 * c + s // 2 + 3)
                    if last and s in (4, 5, 6):
                        mix_split(0, s - 4)
                    if s == 8 or (last and s == 7):
                        for t in range(2):
                            dve.wait_ge(gate_tanh, 2 * c + t + 1)
                            ins = nc.vector.scalar_tensor_tensor(out=gate[:, t, :], in0=gate[:, t, :], scalar=1.0,
                                                                 in1=bank[2 + t][:], op0=ALU.add, op1=ALU.mult)
                        ins.then_inc(gate_ready, 1)
                if not last:
                    kz_build(c + 1, (c + 1) // 2)
                    q_kept(c + 1)
                    v_build(c + 1, (c + 1) // 2)

            with dve.Fori(0, CHUNKS - 1) as c:
                att_body(c, False)
            att_body(CHUNKS - 1, True)

            def copies(layer, st, n):
                y = h if layer == 0 else y2
                dve.wait_ge(o_squared, 16 * layer + 4 * n + st + 1)
                nc.vector.tensor_tensor(y[:, st, ds(512 * n, 512)], bank[st][:], gain_post[:, ds(512 * n, 512)],
                                        ALU.mult).then_inc(o_copied, 1)

            def total(kind, st, first):
                n = root_count(kind, st)
                nc.vector.tensor_reduce(stat[:, 60 + n:61 + n], stat[:, first:first + 4], AX_X, ALU.add)\
                    .then_inc(sum_done, 1)

            def residual(layer, st):
                kind = "C" if layer else "A"
                rstd = reciprocal_root(kind, st, 80 + root_count(kind, st))
                dve.wait_ge(o_copied, 16 * layer + 13 + st)
                if layer == 0:
                    dve.wait_ge(again_landed[st % 2], 16 * (st // 2 + 1))
                for j in range(4):
                    cols = slice(512 * j, 512 * j + 512)
                    y, other = (y2[:, st, cols], h[:, st, cols]) if layer else (h[:, st, cols], x_again[st % 2][:, cols])
                    nc.vector.scalar_tensor_tensor(out=h[:, st, cols], in0=y, scalar=rstd, in1=other,
                                                   op0=ALU.mult, op1=ALU.add).then_inc(h_ready, 1)

            def next_norm(st):
                rstd = reciprocal_root("B", st, 80 + root_count("B", st))
                for j in range(4):
                    at = un[:, st % 2, 512 * j:512 * j + 512]
                    dve.wait_ge(hg_done, 4 * st + j + 1)
                    nc.vector.tensor_scalar(at, at, rstd, None, ALU.mult).then_inc(un_ready, 1)
                norm_turned(ST + st)

            def out_phase(layer, u0, extra):
                for p in range(8):
                    extra(p)
                    if p < 4:
                        mix_split(layer, p + 3)
                    if p == 5:
                        mix_split(layer, 7)
                    split(u0 + p + 3)
                dve.wait_ge(post_landed, 16 * (layer + 1))
                with dve.Fori(1, 3) as n:
                    for p in range(8):
                        if p == 0:
                            for st in range(ST):
                                copies(layer, st, n - 1)
                        split_lo((u0 + p + 3) % DEPTH, u0 + 8 * n + p + 3)
                for half in range(2):
                    for p in range(8):
                        u = u0 + 24 + 8 * half + p + 3
                        if half == 0 and p == 0:
                            for st in range(ST):
                                copies(layer, st, 2)
                        if half == 1 and p == 0:
                            copies(layer, 0, 3)
                            copies(layer, 1, 3)
                        if u < (U_LRU + 3 if layer == 0 else UNITS):
                            split(u)
                        if half == 1 and p in (0, 3):
                            st = p // 3
                            total("C" if layer else "A", st, 8 + 4 * st)
                            residual(layer, st)
                        if layer == 0 and half == 1 and p in (2, 5):
                            st = p // 5
                            dve.wait_ge(sq_done, ST + 4 * st + 4)
                            total("B", st, 100 + 4 * st)
                            next_norm(st)
                copies(layer, 2, 3)
                copies(layer, 3, 3)
                total("C" if layer else "A", 2, 16)
                total("C" if layer else "A", 3, 20)
                residual(layer, 2)
                residual(layer, 3)
                if layer == 0:
                    for st in (2, 3):
                        dve.wait_ge(sq_done, ST + 4 * st + 4)
                        total("B", st, 100 + 4 * st)
                        next_norm(st)

            def att_tail(p):
                for s in (8 + 2 * p, 9 + 2 * p):
                    att_slot(CHUNKS - 1, s)

            out_phase(0, U_O1, att_tail)

            for p in range(3):
                split(U_LRU + p + 3)

            def lru_body(j, last):
                def next_split(p):
                    split_lo((4 + p + 2) % LRU_DEPTH if not last else slot(U_LRU + 4 + 9 * j + p + 2),
                             U_LRU + 4 + 9 * j + p + 2)

                dve.wait_ge(conv_begun, 2 * j + 2)
                for back in (1, 2, 3):
                    if back > 1:
                        dve.wait_ge(conv_tap, 6 * j + 2 * back - 2)
                    for t in range(2):
                        nc.vector.scalar_tensor_tensor(
                            out=xc[:, t, back:SEQ], in0=bank[t][:, 0:SEQ - back],
                            scalar=vec[:, ds(CONV_W + (3 - back) * KT + 2 * j + t, 1)], in1=xc[:, t, back:SEQ],
                            op0=ALU.mult, op1=ALU.add).then_inc(conv_tap, 1)
                next_split(0)
                dve.wait_ge(xc_hi_done, j + 1)
                nc.vector.tensor_tensor(xc_lo[:], xc[:], xc_hi[:].bitcast(F32), ALU.subtract).then_inc(xc_lo_done, 1)
                for p in (1, 2, 3):
                    next_split(p)
                silu = lgate_last if last else lgate
                for t in range(2):
                    dve.wait_ge(lgate_tanh, 2 * j + t + 1)
                    nc.vector.scalar_tensor_tensor(out=silu[:, t, :], in0=silu[:, t, :], scalar=1.0,
                                                   in1=bank[2 + t][:], op0=ALU.add, op1=ALU.mult)\
                        .then_inc(lgate_ready, 1)
                next_split(4)
                if last:
                    for w in range(3):
                        mix_split(1, w)
                dve.wait_ge(t_done, 2 * j + 2)
                nc.vector.tensor_scalar(decay[:], rg[:], 1.0, None, ALU.add).then_inc(one_plus_t, 1)
                if not last:
                    next_split(5)
                dve.wait_ge(one_plus_t, j + 1)
                for t in range(2):
                    nc.vector.reciprocal(decay[:, t, :], decay[:, t, :]).then_inc(q_recip, 1)
                    if t == 0 and not last:
                        next_split(6)
                dve.wait_ge(q_recip, 2 * j + 2)
                dve.wait_ge(root_t_done, j + 1)
                nc.vector.tensor_tensor(bt[:], bt[:], decay[:], ALU.mult).then_inc(b_step, 1)
                dve.wait_ge(b_step, 2 * j + 1)
                nc.vector.tensor_scalar(decay[:], decay[:], 2.0, -1.0, ALU.mult, ALU.add).then_inc(a_done, 1)
                if not last:
                    next_split(7)
                dve.wait_ge(ix_done, j + 2)
                nc.vector.tensor_tensor(bt[:], bt[:], ig[:], ALU.mult).then_inc(b_step, 1)
                dve.wait_ge(a_done, j + 1)
                dve.wait_ge(b_step, 2 * j + 2)
                for t in range(2):
                    nc.vector.tensor_tensor_scan(rg[:, t, :], decay[:, t, :], bt[:, t, :], 0.0, ALU.mult, ALU.add)\
                        .then_inc(scan_done, 1)
                if not last:
                    next_split(8)
                dve.wait_ge(scan_done, 2 * j + 2)
                dve.wait_ge(lgate_ready, 2 * j + 2)
                nc.vector.scalar_tensor_tensor(out=mix[:, ds(2 * j, 2), :], in0=rg[:], scalar=0.5, in1=silu[:],
                                               op0=ALU.mult, op1=ALU.mult).then_inc(lmix_ready, 1)

            with dve.Fori(0, CHUNKS - 1) as j:
                lru_body(j, False)
            lru_body(CHUNKS - 1, True)
            split(U_O2 + 2)
            out_phase(1, U_O2, lambda p: None)

        @block.tensor
        def _(pe):
            def weights(s):
                return (w_hi[:, s, :].rearrange("p (k n) -> p k n", n=256),
                        w_lo[:, s, :].rearrange("p (k n) -> p k n", n=256))

            def three(out_ap, lhs_hi, lhs_lo, rhs_hi, rhs_lo, start, stop, shared=False):
                pe.matmul(out_ap, lhs_hi, rhs_hi, start=start, stop=False, skip_group_check=shared)
                pe.matmul(out_ap, lhs_hi, rhs_lo, start=False, stop=False, skip_group_check=shared)
                return pe.matmul(out_ap, lhs_lo, rhs_hi, start=False, stop=stop, skip_group_check=shared)

            def project_half(s, part, tile, half):
                hi, lo = weights(s)
                tokens = slice(256 * half, 256 * half + 256)
                for kk in range(4):
                    kt = 4 * part + kk
                    cols = slice(tile * P, (tile + 1) * P)
                    ins = three(bank[tile][:, tokens], hi[:, kk, cols], lo[:, kk, cols], u_hi[:, kt, tokens],
                                u_lo[:, kt, tokens], kt == 0 and half == 0, False, shared=True)
                return ins

            def project(s, part, banks, tile, shared=False):
                hi, lo = weights(s)
                for kk in range(4):
                    kt = 4 * part + kk
                    cols = slice(tile * P, (tile + 1) * P)
                    ins = three(bank[banks + tile][:], hi[:, kk, cols], lo[:, kk, cols], u_hi[:, kt, :],
                                u_lo[:, kt, :], kt == 0, kt == KT - 1, shared)
                return ins

            def turn(m):
                for j in range(4):
                    g = 4 * m + j
                    pe.wait_ge(un_ready, g + 1)
                    if g >= 4:
                        pe.wait_ge(u_lo_done, g - 3)
                    for k in range(4):
                        ins = pe.transpose(bank[4 + j][:, k * P:(k + 1) * P],
                                           un[:, m % 2, (4 * j + k) * P:(4 * j + k + 1) * P], ident[:])
                    ins.then_inc(u_turned, 1)

            pe.wait_ge(consts_ready, 7)
            pe.wait_ge(row_landed, 16)
            for j in range(4):
                pe.matmul(bank[j][:], ones_row[:], gain_row[:, 512 * j:512 * j + 512], start=True, stop=True)\
                    .then_inc(gain_spread, 1)
            for st in range(ST):
                turn(st)
                pe.wait_ge(u_lo_done, 4 * st + 4)
                if st == 0:
                    pe.wait_ge(gain_kept, 4)
                cols = slice(st * P, (st + 1) * P)
                for j in range(4):
                    pe.wait_ge(lo_done, U_V + j + 1)
                    hi, lo = weights(slot(U_V + j))
                    for kk in range(4):
                        kt = 4 * j + kk
                        ins = three(bank[st][:, 0:KV_W], u_hi[:, kt, cols], u_lo[:, kt, cols], hi[:, kk, :],
                                    lo[:, kk, :], kt == 0, kt == KT - 1)
                    if st == ST - 1:
                        ins.then_inc(weights_used, 1)
                    elif j == 3:
                        ins.then_inc(v_proj, 1)
            for j in range(4):
                pe.wait_ge(lo_done, U_K + j + 1)
                for tile in range(2):
                    ins = project(slot(U_K + j), j, 4, tile)
                ins.then_inc(weights_used, 1)
            pe.wait_ge(small_landed, 16 * 6)
            pe.transpose(bank[6][:, 0:P], vec_rows[:], ident[:]).then_inc(vec_turned, 1)
            pe.wait_ge(v_kept, 4)
            for j in range(4):
                pe.wait_ge(lo_done, U_Q + j + 1)
                for tile in range(2):
                    ins = project(slot(U_Q + j), j, 0, tile)
                    if tile:
                        ins.then_inc(weights_used, 1)
                    elif j == 3:
                        ins.then_inc(q_proj, 1)

            def scores(c, b):
                w = P if b == 0 else 2 * P
                k0 = max(b - 1, 0) * P
                if b == 0:
                    pe.wait_ge(q_lo_done, 2 * c + 2)
                    pe.wait_ge(kz_lo_done, 2 * c + 2)
                    pe.wait_ge(vec_ready, 1)
                else:
                    pe.wait_ge(scores_masked, 2 * (4 * c + b))
                for t in range(2):
                    q = slice(b * P, (b + 1) * P)
                    keys = slice(k0, k0 + w)
                    ins = three(bank[4 + t][:, 0:2 * w].rearrange("p (h k) -> p h k", h=2), q_hi[:, t, q],
                                q_lo[:, t, q], kz_hi[:, :, keys], kz_lo[:, :, keys], True, True)
                ins.then_inc(scores_done, 1)

            def turn_probs(c, b, k):
                if b == 0 or k == 0:
                    pe.wait_ge(probs_ready, 4 * c + b + 1)
                if b:
                    pe.wait_ge(pt_lo_done, t_index(c, b, k))
                at = 0 if b == 0 else k * P
                for hd in range(4):
                    ins = pe.transpose(bank[6][:, hd * P:(hd + 1) * P], probs[:, b % 2, hd, at:at + P], ident[:])
                ins.then_inc(p_turned, 1)

            def weigh_values(c, b):
                if b == 0:
                    pe.wait_ge(v_lo_done, 2 * c + 2)
                    pe.wait_ge(mix_ready, c + 1)
                else:
                    pe.wait_ge(pv_read, 4 * c + b)
                pe.wait_ge(pt_lo_done, t_index(c, b, 1) + 1)
                for k in ((1,) if b == 0 else (0, 1)):
                    kb = b - 1 + k
                    ins = three(bank[7][:], v_hi[:, kb, :], v_lo[:, kb, :], pt_hi[:, k, :], pt_lo[:, k, :],
                                b == 0 or k == 0, k == 1)
                ins.then_inc(pv_done, 1)

            def att_slot(c, s):
                for step in ATT_STEPS.get(s, ()):
                    if step[0] == "S":
                        scores(c, step[1])
                    elif step[0] == "T":
                        turn_probs(c, step[1], step[2])
                    else:
                        weigh_values(c, step[1])

            def att_body(c, last):
                for p in range(4 if last else 8):
                    pe.wait_ge(lo_done, U_ATT + 8 * c + p + 1)
                    gates = p < 4
                    if p == 0:
                        pe.wait_ge(gate_ready, c + 1)
                    if p == 4:
                        pe.wait_ge(q_lo_done, 2 * c + 2)
                    for tile in range(2):
                        ins = project(p % DEPTH, p % 4, 2 if gates else 0, tile)
                        if tile:
                            ins.then_inc(weights_used, 1)
                        elif p % 4 == 3:
                            ins.then_inc(gate_proj if gates else q_proj, 1)
                        att_slot(c, 2 * p + tile)

            with pe.Fori(0, CHUNKS - 1) as c:
                att_body(c, False)
            att_body(CHUNKS - 1, True)

            def out_unit(s, p, tiles, done):
                hi = w_hi[:, s, :].rearrange("p (k n) -> p k n", n=512)
                lo = w_lo[:, s, :].rearrange("p (k n) -> p k n", n=512)
                for st in tiles:
                    cols = slice(st * P, (st + 1) * P)
                    for kk in range(2):
                        kt = 2 * p + kk
                        ins = three(bank[st][:], u_hi[:, kt, cols], u_lo[:, kt, cols], hi[:, kk, :], lo[:, kk, :],
                                    kt == 0, kt == KT - 1)
                    if st == tiles[-1]:
                        ins.then_inc(weights_used, 1)
                    elif p == 7:
                        ins.then_inc(o_done, 1)
                    done(st)

            def out_phase(layer, u0):
                b0 = 16 * layer
                for p in range(8):
                    pe.wait_ge(lo_done, u0 + p + 1)
                    pe.wait_ge(mix_lo, CHUNKS * layer + p + 1)

                    def attention(st, p=p):
                        if layer == 0 and st % 2 and p < 4:
                            att_slot(CHUNKS - 1, 8 + 2 * p + st // 2)
                    out_unit((u0 + p) % DEPTH, p, range(ST), attention)
                with pe.Fori(1, 3) as n:
                    for p in range(8):
                        pe.wait_ge(lo_done, u0 + 8 * n + p + 1)

                        if p == 0:
                            pe.wait_ge(o_copied, b0 + 4 * n - 3)

                        def copied(st, p=p):
                            if p == 0 and st < ST - 1:
                                pe.wait_ge(o_copied, b0 + 4 * n - 3 + st + 1)
                        out_unit((u0 + p) % DEPTH, p, range(ST), copied)
                for half in range(2):
                    for p in range(8):
                        pe.wait_ge(lo_done, u0 + 24 + 8 * half + p + 1)
                        if p == 0:
                            pe.wait_ge(o_copied, b0 + 10 + 2 * half)
                        out_unit((u0 + p) % DEPTH, p, range(2 * half, 2 * half + 2), lambda st: None)
                        if layer == 0 and half == 1 and p in (5, 7):
                            turn(ST + (p - 5) // 2)

            pe.wait_ge(q_lo_done, 2 * CHUNKS)
            pe.wait_ge(gate_ready, CHUNKS + 1)
            out_phase(0, U_O1)

            pe.wait_ge(u_lo_done, 4 * (ST + 2))
            for j in range(3):
                pe.wait_ge(lo_done, U_LRU + j + 1)
                for tile in range(2):
                    project_half(slot(U_LRU + j), j, tile, 0)
                if j:
                    turn(ST + 1 + j)
            pe.wait_ge(u_lo_done, 8 * ST)
            for j in range(3):
                for tile in range(2):
                    ins = project_half(slot(U_LRU + j), j, tile, 1)
                ins.then_inc(weights_used, 1)
            pe.wait_ge(lo_done, U_LRU + 4)
            project(slot(U_LRU + 3), 3, 0, 0, shared=True).then_inc(xb_proj, 1)
            project(slot(U_LRU + 3), 3, 0, 1, shared=True).then_inc(weights_used, 1)
            pe.wait_ge(o_copied, 16)

            def lru_body(j, last):
                for p in range(5 if last else 9):
                    s = (4 + p) % LRU_DEPTH
                    pe.wait_ge(lo_done, U_LRU + 4 + 9 * j + p + 1)
                    if p == 4:
                        pe.wait_ge(xc_lo_done, j + 1)
                        hi, lo = weights(s)
                        for g in range(2):
                            for tile in range(2):
                                cols = slice(tile * P, (tile + 1) * P)
                                for kk in range(2):
                                    ins = three(bank[4 + 2 * g + tile][:], hi[:, 2 * g + kk, cols],
                                                lo[:, 2 * g + kk, cols], xc_hi[:, kk, :], xc_lo[:, kk, :],
                                                kk == 0, kk == 1)
                                if g and tile:
                                    ins.then_inc(weights_used, 1)
                                else:
                                    ins.then_inc(ri_proj, 1)
                        continue
                    gates = p < 4
                    if p == 5:
                        pe.wait_ge(conv_tap, 6 * j + 6)
                    for tile in range(2):
                        ins = project(s, p if gates else p - 5, 2 if gates else 0, tile)
                        if tile:
                            ins.then_inc(weights_used, 1)
                        elif p in (3, 8):
                            ins.then_inc(lgate_proj if gates else xb_proj, 1)
                pe.wait_ge(lgate_ready, 2 * j + 2)

            with pe.Fori(0, CHUNKS - 1) as j:
                lru_body(j, False)
            lru_body(CHUNKS - 1, True)
            pe.wait_ge(conv_tap, 6 * CHUNKS)
            out_phase(1, U_O2)


def program(nc, a, out):
    rows = lambda ap, spec, **k: ap.rearrange(spec, **k)
    build(
        nc,
        rows(a["x"], "b s d -> (b s) d"), a["norm_pre"], a["norm_post"],
        rows(a["attn_w_in"], "a k n -> (a k) n"), rows(a["attn_w_out"], "a k n -> (a k) n"), a["attn_sinks"],
        rows(a["lru_w_in"], "a k n -> (a k) n"),
        rows(a["lru_conv_w"], "a c (t p) -> (a c t) p", p=P), rows(a["lru_conv_b"], "a (t p) -> (a t) p", p=P),
        rows(a["lru_w_a"], "a g i o -> (a g i) o"), rows(a["lru_b_a"], "a g (t p) -> (a g t) p", p=P),
        rows(a["lru_w_x"], "a g i o -> (a g i) o"), rows(a["lru_b_x"], "a g (t p) -> (a g t) p", p=P),
        rows(a["lru_lambda"], "a (t p) -> (a t) p", p=P),
        rows(a["lru_w_out"], "a k n -> (a k) n"),
        rows(out, "b s d -> (b s) d"),
    )


INPUTS = ["x", "norm_pre", "norm_post", "attn_w_in", "attn_w_out", "attn_sinks", "lru_w_in", "lru_conv_w",
          "lru_conv_b", "lru_w_a", "lru_b_a", "lru_w_x", "lru_b_x", "lru_lambda", "lru_w_out"]


def kernel(**inputs):
    import numpy as np
    import concourse.bacc as bacc
    from concourse.bass_utils import run_bass_kernel_spmd

    nc = bacc.Bacc("TRN2", target_bir_lowering=False, num_devices=1)
    arrays, args = {}, {}
    for name in INPUTS:
        a = np.ascontiguousarray(inputs[name])
        arrays[f"in_{name}"] = a
        args[name] = nc.dram_tensor(f"in_{name}", a.shape, mybir.dt.from_np(a.dtype), kind="ExternalInput").ap()
    out = nc.dram_tensor("out", (1, SEQ, D), F32, kind="ExternalOutput").ap()
    program(nc, args, out)
    return run_bass_kernel_spmd(nc, [arrays], core_ids=[0]).results[0]["out"]
```

```python
from contextlib import ExitStack

import concourse.bass as bass
from concourse import mybir

F32 = mybir.dt.float32
F32R = mybir.dt.float32r
ALU = mybir.AluOpType
ACT = mybir.ActivationFunctionType
AX_X = mybir.AxisListType.X
ds = bass.ds

P = 128
SEQ = 512
D = 2048
KT = D // P
ST = SEQ // P
HEAD = 64
HEADS = D // HEAD
KV_HEADS = HEADS // 8
KV_W = KV_HEADS * HEAD
CHUNKS = D // 256
NB = SEQ // P
EPS = 1e-6
MASKED = -1e30
CONV = 4
LRU_BW = 256

DEPTH = 4
LRU_DEPTH = 3
U_V, U_K, U_Q = 0, 4, 8
U_ATT = 12
U_O1 = U_ATT + 8 * CHUNKS - 4
U_LRU = U_O1 + 40
U_O2 = U_LRU + 9 * CHUNKS
UNITS = U_O2 + 40

ATT_STEPS = {1: [("S", 0)], 3: [("S", 1)], 5: [("T", 0, 1)], 6: [("S", 2)], 7: [("V", 0), ("T", 1, 0)],
             8: [("T", 1, 1)], 9: [("S", 3)], 10: [("V", 1), ("T", 2, 0)], 11: [("T", 2, 1)],
             13: [("V", 2), ("T", 3, 0)], 14: [("T", 3, 1)], 15: [("V", 3)]}

TOGETHER = 5
EARLY = 3

ROOTS = ([("x", st) for st in range(4)]
         + [("A", 0), ("A", 1), ("B", 0), ("B", 1), ("A", 2), ("A", 3), ("B", 2), ("B", 3)]
         + [("C", st) for st in range(4)])


def t_index(c, b, k):
    return 7 * c + (0 if b == 0 else 2 * b - 1 + k)


def root_count(kind, st):
    return ROOTS.index((kind, st)) + 1


def depth(u):
    return DEPTH if u < U_LRU + 4 or u > U_O2 + 2 else LRU_DEPTH


def slot(u):
    return (u - U_LRU) % LRU_DEPTH if U_LRU + 4 <= u < U_O2 else u % DEPTH


def landed(u):
    n = 0
    for v in range(u + 1):
        if slot(v) == slot(u):
            n += 16
            if U_LRU <= v < U_O2 and (v - U_LRU) % 9 == 8:
                n += 16
    return n


def build(nc, x, norm_pre, norm_post, w_in, w_out, sinks, l_in, conv_w, conv_b, w_a, b_a, w_x, b_x,
          lam, l_out, out):
    ctx = ExitStack()
    with ctx:
        base = (nc.sbuf_base + 63) // 64 * 64
        cursor = [base]

        def place(name, shape, dt, at=None):
            size = 4
            for n in shape[1:]:
                size *= n
            if at is None:
                at = cursor[0]
                cursor[0] += (size + 31) // 32 * 32
            return nc.alloc_sbuf_tensor_at(name, shape, dt, offset=at)

        def sem(name):
            return ctx.enter_context(nc.semaphore(name))

        u_hi = place("u_hi", [P, KT, SEQ], F32R)
        u_lo = place("u_lo", [P, KT, SEQ], F32R)
        y_at = cursor[0]
        mix = place("mix", [P, KT, SEQ], F32)
        h_at = cursor[0]
        h = place("h", [P, ST, D], F32)
        raw_at = cursor[0]
        raw = place("raw", [P, DEPTH, 1024], F32)
        w_hi = place("w_hi", [P, DEPTH, 1024], F32R)
        w_lo = place("w_lo", [P, DEPTH, 1024], F32R)
        ident = place("ident", [P, P], F32)
        vec = place("vec", [P, P], F32)
        mask = place("mask", [P, 2 * P], F32)
        nsink = place("nsink", [P, HEADS], F32)
        eps = place("eps", [P, 1], F32)
        stat = place("stat", [P, 128], F32)
        soft = place("soft", [P, 6, KT], F32)
        sp4 = place("sp4", [P, KT], F32)
        row_max = place("row_max", [P, 2, 4], F32)
        shift = place("shift", [P, 2, 4], F32)
        sink_shift = place("sink_shift", [P, 2, 4], F32)
        row_sum = place("row_sum", [P, 2, 4], F32)
        sink_exp = place("sink_exp", [P, 2, 4], F32)
        denom = place("denom", [P, 2, 4], F32)
        t_at = (cursor[0] + 63) // 64 * 64
        assert t_at + 7 * 4096 <= nc.sbuf_usable_end, (t_at, nc.sbuf_usable_end)
        K = 1024
        gain_pre = place("gain_pre", [P, D], F32, y_at)
        un = place("un", [P, 2, D], F32, y_at + 8 * K)
        square = place("square", [P, D], F32, t_at)
        gain_post = place("gain_post", [P, D], F32, t_at + 8 * K)
        x_again = [place(f"x_again{i}", [P, D], F32, t_at + 16 * K * i) for i in range(2)]
        dump = place("dump", [P, SEQ], F32, t_at + 24 * K)
        vec_rows = place("vec_rows", [P, P], F32, t_at + 26 * K)
        gain_row = place("gain_row", [1, D], F32, t_at + 16 * K)
        ones_row = place("ones_row", [1, P], F32, t_at + 27 * K)
        y2 = place("y2", [P, ST, D], F32, y_at)
        kc = place("kc", [P, KV_HEADS, SEQ], F32, h_at)
        probs = place("probs", [P, 2, 4, 2 * P], F32, h_at + 8 * K)
        kg_hi = place("kg_hi", [P, SEQ], F32R, h_at + 16 * K)
        kg_lo = place("kg_lo", [P, SEQ], F32R, h_at + 18 * K)
        pt_hi = place("pt_hi", [P, 2, SEQ], F32R, h_at + 24 * K)
        pt_lo = place("pt_lo", [P, 2, SEQ], F32R, h_at + 28 * K)
        q_both = place("q_both", [P, 4, SEQ], F32R, t_at)
        gate = place("gate", [P, 2, SEQ], F32, t_at + 8 * K)
        v_both = place("v_both", [P, NB, P], F32R, t_at + 12 * K)
        pv_low = place("pv_low", [HEAD, SEQ], F32, t_at + 14 * K)
        vc = place("vc", [P, NB, KV_W], F32, t_at + 16 * K)
        xc = place("xc", [P, 2, SEQ], F32, t_at)
        xc_hi = place("xc_hi", [P, 2, SEQ], F32R, t_at + 4 * K)
        xc_lo = place("xc_lo", [P, 2, SEQ], F32R, t_at + 8 * K)
        rg = place("rg", [P, 2, SEQ], F32, t_at + 12 * K)
        bt = place("bt", [P, 2, SEQ], F32, t_at + 16 * K)
        ig = place("ig", [P, 2, SEQ], F32, t_at + 20 * K)
        decay = place("decay", [P, 2, SEQ], F32, t_at + 24 * K)
        lgate = place("lgate", [P, 2, SEQ], F32, raw_at + 3 * 4 * K)
        lgate_last = place("lgate_last", [P, 2, SEQ], F32, base + 14 * 2 * K)
        bank = [ctx.enter_context(nc.psum_tensor(f"bank{i}", [P, 512], F32)) for i in range(8)]

        x_landed = [sem(f"x_landed{i}") for i in range(ST)]
        small_landed = sem("small_landed")
        row_landed = sem("row_landed")
        gain_spread = sem("gain_spread")
        gain_kept = sem("gain_kept")
        pre2_landed = sem("pre2_landed")
        post_landed = sem("post_landed")
        again_landed = [sem(f"again_landed{i}") for i in range(2)]
        raw_landed = [sem(f"raw_landed{i}") for i in range(DEPTH)]
        hi_done = sem("hi_done")
        lo_done = sem("lo_done")
        weights_used = sem("weights_used")
        consts_ready = sem("consts_ready")
        vec_turned = sem("vec_turned")
        vec_ready = sem("vec_ready")
        soft_step = sem("soft_step")
        soft_exp = sem("soft_exp")
        sq_done = sem("sq_done")
        root_done = sem("root_done")
        sum_done = sem("sum_done")
        rstd_done = sem("rstd_done")
        hg_done = sem("hg_done")
        h_ready = sem("h_ready")
        un_ready = sem("un_ready")
        u_turned = sem("u_turned")
        u_hi_done = sem("u_hi_done")
        u_lo_done = sem("u_lo_done")
        v_proj = sem("v_proj")
        k_kept = sem("k_kept")
        v_kept = sem("v_kept")
        q_proj = sem("q_proj")
        q_hi_done = sem("q_hi_done")
        q_lo_done = sem("q_lo_done")
        gate_proj = sem("gate_proj")
        gate_tanh = sem("gate_tanh")
        gate_ready = sem("gate_ready")
        kg_hi_done = sem("kg_hi_done")
        kg_lo_done = sem("kg_lo_done")
        v_hi_done = sem("v_hi_done")
        v_lo_done = sem("v_lo_done")
        scores_done = sem("scores_done")
        scores_masked = sem("scores_masked")
        max_done = sem("max_done")
        shift_done = sem("shift_done")
        sink_shift_done = sem("sink_shift_done")
        exp_done = sem("exp_done")
        denom_done = sem("denom_done")
        recip_done = sem("recip_done")
        probs_ready = sem("probs_ready")
        p_turned = sem("p_turned")
        pt_hi_done = sem("pt_hi_done")
        pt_lo_done = sem("pt_lo_done")
        pv_done = sem("pv_done")
        pv_low_kept = sem("pv_low_kept")
        pv_read = sem("pv_read")
        mix_ready = sem("mix_ready")
        mix_hi = sem("mix_hi")
        mix_lo = sem("mix_lo")
        o_done = sem("o_done")
        o_copied = sem("o_copied")
        o_squared = sem("o_squared")
        xb_proj = sem("xb_proj")
        conv_begun = sem("conv_begun")
        conv_tap = sem("conv_tap")
        xc_hi_done = sem("xc_hi_done")
        xc_lo_done = sem("xc_lo_done")
        lgate_proj = sem("lgate_proj")
        lgate_tanh = sem("lgate_tanh")
        lgate_ready = sem("lgate_ready")
        ri_proj = sem("ri_proj")
        r_done = sem("r_done")
        i_done = sem("i_done")
        t_done = sem("t_done")
        root_t_done = sem("root_t_done")
        one_plus_t = sem("one_plus_t")
        q_recip = sem("q_recip")
        b_step = sem("b_step")
        a_done = sem("a_done")
        ix_done = sem("ix_done")
        scan_done = sem("scan_done")
        lmix_ready = sem("lmix_ready")
        last_part_scaled = sem("last_part_scaled")
        last_part_ready = sem("last_part_ready")
        stored = sem("stored")

        LAM, B_A, B_X, CONV_B, CONV_W = 0, 16, 32, 48, 64

        def w_unit(w, row0, kts, col0, cols):
            return w[ds(row0, kts * P), ds(col0, cols)].rearrange("(k p) n -> p k n", p=P)

        def bcast(ap, shape):
            return ap.to_broadcast(shape)

        block = ctx.enter_context(nc.Block())

        @block.sync
        def _(sp):
            def load(s, u, free_after, src):
                if free_after is not None:
                    sp.wait_ge(lo_done, free_after)
                dst = raw[:, s, :].rearrange("p (k n) -> p k n", n=src[0].shape[2])
                at = 0
                for part in src:
                    k = part.shape[1]
                    sp.dma_start(dst[:, at:at + k, :], part).then_inc(raw_landed[s], 16)
                    at += k

            def free(u):
                return u - depth(u) + 1 if u >= depth(u) else None

            def load_x(st):
                sp.dma_start(h[:, st, :], x[st * P:(st + 1) * P, :]).then_inc(x_landed[st], 16)

            def load_kv(u0, j, col0):
                load(slot(u0 + j), u0 + j, free(u0 + j), [w_unit(w_in, j * 512, 4, col0, 256)])

            sp.dma_start(gain_row[:], norm_pre[0:1, :]).then_inc(row_landed, 16)
            load_x(0)
            load_kv(U_V, 0, D + KV_W)
            load_kv(U_V, 1, D + KV_W)
            load_x(1)
            load_kv(U_V, 2, D + KV_W)
            load_kv(U_V, 3, D + KV_W)
            load_x(2)
            load_x(3)
            sp.dma_start(nsink[:], sinks.to_broadcast([P, HEADS])).then_inc(small_landed, 16)
            rows = [(lam, LAM, 1), (b_a, B_A, 1), (b_x, B_X, 1), (conv_b, CONV_B, 1), (conv_w, CONV_W, CONV)]
            for v, r0, n in rows:
                sp.dma_start(vec_rows[r0:r0 + n * KT, :], v).then_inc(small_landed, 16)
            for j in range(4):
                load_kv(U_K, j, D)
            for j in range(4):
                load_kv(U_Q, j, 0)

            def att_units(i, last):
                g0 = D + 2 * KV_W
                for p in range(4 if last else 8):
                    u = U_ATT + 8 * i + p
                    src = w_unit(w_in, (p % 4) * 512, 4, g0 + 256 * i if p < 4 else 256 * i + 256, 256)
                    load(p % DEPTH, u, u - DEPTH + 1, [src])

            with sp.Fori(0, CHUNKS - 1) as i:
                att_units(i, False)
            att_units(CHUNKS - 1, True)

            def out_units(w, u0):
                def chunk(n, u0n, frees):
                    for p in range(8):
                        if isinstance(n, int) and n == 0 and p == 3 and u0 == U_O2:
                            sp.wait_ge(lmix_ready, CHUNKS - 1)
                        load(p % DEPTH, u0n + p, frees(p), [w_unit(w, p * 256, 2, 512 * n, 512)])
                chunk(0, u0, lambda p: free(u0 + p))
                with sp.Fori(1, 3) as n:
                    chunk(n, u0 + 8 * n, lambda p: u0 + 8 * n + p - DEPTH + 1)
                for half in range(2):
                    chunk(3, u0 + 24 + 8 * half, lambda p: free(u0 + 24 + 8 * half + p))

            out_units(w_out, U_O1)

            def lru_units(j, last):
                for p in range(5 if last else 9):
                    u = U_LRU + 4 + 9 * j + p
                    if p < 4:
                        src = [w_unit(l_in, p * 512, 4, D + 256 * j, 256)]
                    elif p == 4:
                        src = [w_unit(w_a, LRU_BW * j, 2, 0, 256), w_unit(w_x, LRU_BW * j, 2, 0, 256)]
                    else:
                        src = [w_unit(l_in, (p - 5) * 512, 4, 256 * j + 256, 256)]
                    load((4 + p) % LRU_DEPTH, u, u - LRU_DEPTH + 1, src)

            for j in range(4):
                load(slot(U_LRU + j), U_LRU + j, free(U_LRU + j), [w_unit(l_in, j * 512, 4, 0, 256)])
            with sp.Fori(0, CHUNKS - 1) as j:
                lru_units(j, False)
            lru_units(CHUNKS - 1, True)
            out_units(l_out, U_O2)

            def store(st, col0, cols):
                at = slice(col0, col0 + cols)
                sp.dma_start(out[st * P:(st + 1) * P, at], h[:, st, at]).then_inc(stored, 16)

            for st in range(ST - 1):
                for half in range(2):
                    sp.wait_ge(h_ready, 4 * (ST + st) + 2 * half + 2)
                    store(st, half * D // 2, D // 2)
            for j in (0, 1, 3, 2):
                if j == 3:
                    sp.wait_ge(last_part_ready, 1)
                else:
                    sp.wait_ge(h_ready, 4 * (2 * ST - 1) + j + 1)
                store(ST - 1, 512 * j, 512)
            sp.wait_ge(stored, 16 * (2 * (ST - 1) + 4))

        @block.gpsimd
        def _(pool):
            nc.gpsimd.memset(ones_row[:], 1.0).then_inc(consts_ready, 1)
            nc.gpsimd.memset(ident[:], 0.0).then_inc(consts_ready, 1)
            nc.gpsimd.memset(mask[:], 0.0).then_inc(consts_ready, 1)
            nc.gpsimd.memset(eps[:], EPS).then_inc(consts_ready, 1)
            pool.wait_ge(consts_ready, 4)
            nc.gpsimd.affine_select(out=ident[:], in_=ident[:], compare_op=ALU.not_equal, fill=1.0, base=0,
                                    pattern=[[-1, P]], channel_multiplier=1).then_inc(consts_ready, 1)
            nc.gpsimd.affine_select(out=mask[:], in_=mask[:], compare_op=ALU.is_ge, fill=MASKED, base=-1,
                                    pattern=[[1, 2 * P]], channel_multiplier=-1).then_inc(consts_ready, 1)
            pool.wait_ge(consts_ready, 6)
            nc.gpsimd.affine_select(out=mask[:], in_=mask[:], compare_op=ALU.is_ge, fill=MASKED, base=P,
                                    pattern=[[-1, 2 * P]], channel_multiplier=1).then_inc(consts_ready, 1)
            nc.gpsimd.memset(stat[:, 127:128], 0.0).then_inc(mix_ready, 1)
            nc.gpsimd.memset(stat[:, 125:126], 0.0).then_inc(ix_done, 1)

            def gate_mix(c):
                pool.wait_ge(pv_read, 4 * c + 4)
                pool.wait_ge(gate_ready, c + 2)
                nc.gpsimd.tensor_tensor(mix[:, ds(2 * c, 2), :], mix[:, ds(2 * c, 2), :], gate[:], ALU.mult)\
                    .then_inc(mix_ready, 1)

            with pool.Fori(0, CHUNKS - 1) as c:
                gate_mix(c)
            gate_mix(CHUNKS - 1)

            pool.wait_ge(mix_ready, CHUNKS + 1)
            pool.dma_start(gain_post[:], norm_post[0:1, :].to_broadcast([P, D])).then_inc(post_landed, 16)
            for st in range(2):
                pool.dma_start(x_again[st][:], x[st * P:(st + 1) * P, :]).then_inc(again_landed[st], 16)
            pool.wait_ge(mix_lo, CHUNKS)
            pool.dma_start(gain_pre[:], norm_pre[1:2, :].to_broadcast([P, D])).then_inc(pre2_landed, 16)
            pool.wait_ge(pre2_landed, 16)
            for st in range(ST):
                if st >= 2:
                    pool.wait_ge(u_turned, 4 * (ST + st - 1))
                for j in range(4):
                    cols = slice(512 * j, 512 * j + 512)
                    pool.wait_ge(h_ready, 4 * st + j + 1)
                    nc.gpsimd.tensor_tensor(un[:, st % 2, cols], h[:, st, cols], gain_pre[:, cols], ALU.mult)\
                        .then_inc(hg_done, 1)
                if st < 2:
                    pool.dma_start(x_again[st][:], x[(st + 2) * P:(st + 3) * P, :]).then_inc(again_landed[st], 16)

            def lru_product(j):
                pool.wait_ge(i_done, j + 1)
                nc.gpsimd.tensor_tensor(ig[:], ig[:], xc[:], ALU.mult).then_inc(ix_done, 1)

            with pool.Fori(0, CHUNKS - 1) as j:
                lru_product(j)
            lru_product(CHUNKS - 1)
            pool.wait_ge(lmix_ready, CHUNKS)
            pool.dma_start(gain_post[:], norm_post[1:2, :].to_broadcast([P, D])).then_inc(post_landed, 16)
            pool.wait_ge(last_part_scaled, 1)
            at = h[:, ST - 1, 1536:D]
            nc.gpsimd.tensor_tensor(at, at, y2[:, ST - 1, 1536:D], ALU.add).then_inc(last_part_ready, 1)

        @block.scalar
        def _(act):
            def split_hi(s, u, landed_at, used):
                act.wait_ge(raw_landed[s], landed_at)
                if used is not None:
                    act.wait_ge(weights_used, used)
                nc.scalar.activation(w_hi[:, s, :], raw[:, s, :], ACT.Copy).then_inc(hi_done, 1)

            def split(u):
                split_hi(slot(u), u, landed(u), u - depth(u) + 1 if u >= depth(u) else None)

            def norm_turned(m, groups=range(4)):
                st = m % ST
                for j in groups:
                    g = 4 * m + j
                    act.wait_ge(u_turned, g + 1)
                    nc.scalar.activation(u_hi[:, 4 * j:4 * j + 4, st * P:(st + 1) * P],
                                         bank[4 + j][:].rearrange("p (k s) -> p k s", k=4), ACT.Copy)\
                        .then_inc(u_hi_done, 1)

            def norm_root(st):
                act.wait_ge(x_landed[st], 16)
                nc.scalar.activation(square[:], h[:, st, :], ACT.Square, accum_out=stat[:, 2 * st:2 * st + 1])\
                    .then_inc(sq_done, 1)
                act.wait_ge(sq_done, st + 1)
                nc.scalar.activation(stat[:, 2 * st + 1:2 * st + 2], stat[:, 2 * st:2 * st + 1], ACT.Sqrt,
                                     bias=eps[:, 0:1], scale=1.0 / D).then_inc(root_done, 1)

            def keep_gain(j):
                act.wait_ge(gain_spread, j + 1)
                nc.scalar.activation(gain_pre[:, 512 * j:512 * j + 512], bank[j][:], ACT.Copy).then_inc(gain_kept, 1)

            act.wait_ge(consts_ready, 4)
            nc.scalar.activation(stat[:, 124:125], eps[:, 0:1], ACT.Sqrt)
            keep_gain(0)
            norm_root(0)
            keep_gain(1)
            keep_gain(2)
            split(U_V)
            keep_gain(3)
            norm_turned(0, range(2))
            split(U_V + 1)
            norm_turned(0, range(2, 4))
            split(U_V + 2)
            norm_root(1)
            split(U_V + 3)
            norm_root(2)
            norm_turned(1)
            norm_root(3)
            norm_turned(2)
            norm_turned(3)
            for j in range(7):
                split(U_K + j)
            act.wait_ge(weights_used, U_K + 4)
            for t in range(2):
                for half in range(2):
                    nc.scalar.activation(kc[64 * half:64 * half + 64, 2 * t + 1, :],
                                         bank[4 + t][64:128, :], ACT.Copy).then_inc(k_kept, 1)

            def kg_build(c, group):
                act.wait_ge(k_kept, 8)
                nc.scalar.activation(kg_hi[:], kc[:, group, :], ACT.Copy).then_inc(kg_hi_done, 1)

            def v_build(c, group):
                act.wait_ge(v_kept, 4)
                nc.scalar.activation(v_both[:, :, 0:HEAD], vc[:, :, ds(group * HEAD, HEAD)], ACT.Copy)\
                    .then_inc(v_hi_done, 1)

            def q_kept(c):
                for t in range(2):
                    if t == 0:
                        act.wait_ge(q_proj, c + 1)
                    else:
                        act.wait_ge(weights_used, U_Q + 4 + 8 * c)
                    for odd in range(2):
                        rows = slice(HEAD * odd, HEAD * odd + HEAD)
                        nc.scalar.activation(q_both[rows, 2 * t + odd, :], bank[t][rows, :], ACT.Copy,
                                             scale=HEAD ** -0.5).then_inc(q_hi_done, 1)

            kg_build(0, 0)
            v_build(0, 0)
            for p in range(4):
                split(U_Q + p + 3)
                if p == 1:
                    act.wait_ge(soft_step, 1)
                    nc.scalar.activation(soft[:, 1, :], soft[:, 0, :], ACT.Exp).then_inc(soft_exp, 1)
            q_kept(0)

            def exps(c, b):
                e = 4 * c + b
                w = P if b == 0 else 2 * P
                act.wait_ge(shift_done, e + 1)
                for hd in range(4):
                    nc.scalar.activation(probs[:, b % 2, hd, 0:w], probs[:, b % 2, hd, 0:w], ACT.Exp,
                                         bias=shift[:, b % 2, hd:hd + 1],
                                         accum_out=row_sum[:, b % 2, hd:hd + 1]).then_inc(exp_done, 1)
                act.wait_ge(sink_shift_done, e + 1)
                nc.scalar.activation(sink_exp[:, b % 2, :], sink_shift[:, b % 2, :], ACT.Exp).then_inc(exp_done, 1)

            def att_slot(c, s):
                for step in ATT_STEPS.get(s, ()):
                    if step[0] == "T":
                        _, b, k = step
                        act.wait_ge(p_turned, t_index(c, b, k) + 1)
                        if b:
                            act.wait_ge(pv_done, 4 * c + b)
                        nc.scalar.activation(pt_hi[:, k, :], bank[6][:], ACT.Copy).then_inc(pt_hi_done, 1)
                    elif step[0] == "V":
                        act.wait_ge(pv_done, 4 * c + step[1] + 1)
                        nc.scalar.activation(pv_low[:], bank[7][HEAD:P, :], ACT.Copy).then_inc(pv_low_kept, 1)
                for step in ATT_STEPS.get(s - 1, ()):
                    if step[0] == "S":
                        exps(c, step[1])

            def mix_split(layer, w):
                act.wait_ge(lmix_ready if layer else mix_ready, w + (1 if layer else 2))
                act.wait_ge(weights_used, (U_O2 - 1 if layer else U_O1) - 3 + w // 2)
                nc.scalar.activation(u_hi[:, 2 * w:2 * w + 2, :], mix[:, 2 * w:2 * w + 2, :], ACT.Copy)\
                    .then_inc(mix_hi, 1)

            def keep_gate(c):
                act.wait_ge(mix_ready, c + 1)
                for t in range(2):
                    if t == 0:
                        act.wait_ge(gate_proj, c + 1)
                    else:
                        act.wait_ge(weights_used, U_ATT + 4 + 8 * c)
                    nc.scalar.activation(gate[:, t, :], bank[2 + t][:], ACT.Tanh, scale=0.5).then_inc(gate_tanh, 1)

            def att_body(c, last):
                for s in range(8 if last else 16):
                    if last and s == 7:
                        keep_gate(c)
                    att_slot(c, s)
                    if s % 2 == 0 and not last:
                        p = s // 2
                        u = U_ATT + 8 * c + p + 3
                        split_hi((p + 3) % DEPTH, u,
                                 16 * (2 * c + (U_ATT + p + 3) // DEPTH + 1), u - DEPTH + 1)
                    elif last and s in (0, 2, 4, 7):
                        split(U_ATT + 8 * c + s // 2 + 3)
                    if last and s in (4, 7):
                        mix_split(0, s // 5)
                    if s == 8:
                        keep_gate(c)
                if not last:
                    act.wait_ge(scores_done, 4 * c + 4)
                    kg_build(c + 1, (c + 1) // 2)
                    q_kept(c + 1)
                    act.wait_ge(pv_done, 4 * c + 4)
                    v_build(c + 1, (c + 1) // 2)

            with act.Fori(0, CHUNKS - 1) as c:
                att_body(c, False)
            att_body(CHUNKS - 1, True)

            def squares(layer, st, n):
                u0 = U_O2 if layer else U_O1
                if isinstance(n, int) and n == 3:
                    if st % 2:
                        act.wait_ge(weights_used, u0 + 24 + 8 * (st // 2) + 8)
                    else:
                        act.wait_ge(o_done, 11 * layer + 10 + st // 2)
                elif st == ST - 1:
                    act.wait_ge(weights_used, u0 + 8 * n + 8)
                else:
                    act.wait_ge(o_done, 11 * layer + 3 * n + st + 1)
                nc.scalar.activation(dump[:], bank[st][:], ACT.Square,
                                     accum_out=stat[:, ds(8 + 4 * st + n, 1)]).then_inc(o_squared, 1)
                act.wait_ge(o_squared, 16 * layer + 4 * n + st + 1)

            def root(kind, st):
                n = root_count(kind, st)
                act.wait_ge(sum_done, n - ST)
                nc.scalar.activation(stat[:, 80 + n:81 + n], stat[:, 60 + n:61 + n], ACT.Sqrt,
                                     bias=eps[:, 0:1], scale=1.0 / D).then_inc(root_done, 1)

            def residual_squares(st):
                for j in range(4):
                    act.wait_ge(h_ready, 4 * st + j + 1)
                    nc.scalar.activation(dump[:], h[:, st, 512 * j:512 * j + 512], ACT.Square,
                                         accum_out=stat[:, 100 + 4 * st + j:101 + 4 * st + j]).then_inc(sq_done, 1)
                    act.wait_ge(sq_done, ST + 4 * st + j + 1)

            def out_phase(layer, u0, extra):
                kind = "C" if layer else "A"
                for p in range(EARLY * layer, 8):
                    extra(p, 0)
                    if p < 6:
                        mix_split(layer, p + 2)
                    split(u0 + p + 3)
                    extra(p, 1)
                with act.Fori(1, 3) as n:
                    for p in range(8):
                        if p == 0:
                            for st in range(ST):
                                squares(layer, st, n - 1)
                        u = u0 + 8 * n + p + 3
                        s = (u0 + p + 3) % DEPTH
                        split_hi(s, u, 32 * n + landed(u0 + 8 + p + 3) - 32, u - DEPTH + 1)
                for p in range(8):
                    if p == 0:
                        for st in range(ST):
                            squares(layer, st, 2)
                    split(u0 + 24 + p + 3)
                first = u0 + 32
                squares(layer, 0, 3)
                squares(layer, 1, 3)
                split(first + 3)
                root(kind, 0)
                root(kind, 1)
                for p in range(4, 8):
                    split(first + p)
                if layer == 0:
                    residual_squares(0)
                    split(U_LRU)
                    root("B", 0)
                    residual_squares(1)
                    root("B", 1)
                    norm_turned(ST)
                squares(layer, 2, 3)
                if layer == 0:
                    norm_turned(ST + 1)
                root(kind, 2)
                if layer == 1:
                    squares(layer, 3, 3)
                    root(kind, 3)
                    n = root_count(kind, 3)
                    act.wait_ge(rstd_done, n)
                    act.wait_ge(o_copied, 32)
                    at = y2[:, ST - 1, 1536:D]
                    nc.scalar.activation(at, at, ACT.Copy, scale=stat[:, 40 + n:41 + n])\
                        .then_inc(last_part_scaled, 1)
                    return
                split(U_LRU + 1)
                squares(layer, 3, 3)
                split(U_LRU + 2)
                split(U_LRU + 3)
                residual_squares(2)
                root(kind, 3)
                root("B", 2)
                residual_squares(3)
                root("B", 3)
                norm_turned(ST + 2)
                norm_turned(ST + 3)

            def att_tail(p, half):
                att_slot(CHUNKS - 1, 8 + 2 * p + half)

            out_phase(0, U_O1, att_tail)

            for p in range(1, 3):
                split(U_LRU + p + 3)

            def lru_body(j, last):
                def next_split(p):
                    if last:
                        split(U_LRU + 4 + 9 * j + p + 2)
                        return
                    u = U_LRU + 4 + 9 * j + p + 2
                    s = (4 + p + 2) % LRU_DEPTH
                    k0 = landed(U_LRU + 4 + p + 2)
                    per = landed(U_LRU + 13 + p + 2) - k0
                    split_hi(s, u, k0 + per * j, u - LRU_DEPTH + 1)

                def column(v, t):
                    return vec[:, ds(v + 2 * j + t, 1)]

                act.wait_ge(vec_ready, 1)
                act.wait_ge(ix_done, j + 1)
                for t in range(2):
                    if t == 0:
                        act.wait_ge(xb_proj, j + 1)
                    else:
                        act.wait_ge(weights_used, U_LRU + 4 + 9 * j)
                    nc.scalar.activation(xc[:, t, :], bank[t][:], ACT.Identity, bias=column(CONV_B, t),
                                         scale=column(CONV_W + 3 * KT, t)).then_inc(conv_begun, 1)
                next_split(0)
                act.wait_ge(conv_tap, 6 * j + 6)
                nc.scalar.activation(xc_hi[:], xc[:], ACT.Copy).then_inc(xc_hi_done, 1)
                for p in (1, 2, 3):
                    next_split(p)
                silu = lgate_last if last else lgate
                for t in range(2):
                    if t == 0 and not last:
                        act.wait_ge(lgate_proj, j + 1)
                    else:
                        act.wait_ge(weights_used, U_LRU + 8 + 9 * j)
                    nc.scalar.activation(silu[:, t, :], bank[2 + t][:], ACT.Tanh, scale=0.5)\
                        .then_inc(lgate_tanh, 1)
                next_split(4)
                if last:
                    for w in range(2):
                        mix_split(1, w)
                for t in range(2):
                    act.wait_ge(ri_proj, 3 * j + t + 1)
                    nc.scalar.activation(rg[:, t, :], bank[4 + t][:], ACT.Sigmoid, bias=column(B_A, t))\
                        .then_inc(r_done, 1)
                for t in range(2):
                    if t == 0:
                        act.wait_ge(ri_proj, 3 * j + 3)
                    else:
                        act.wait_ge(weights_used, U_LRU + 9 + 9 * j)
                    ins = nc.scalar.activation(ig[:, t, :], bank[6 + t][:], ACT.Sigmoid, bias=column(B_X, t))
                ins.then_inc(i_done, 1)
                act.wait_ge(r_done, 2 * j + 2)
                for t in range(2):
                    nc.scalar.activation(rg[:, t, :], rg[:, t, :], ACT.Tanh, scale=sp4[:, ds(2 * j + t, 1)])\
                        .then_inc(t_done, 1)
                if not last:
                    next_split(5)
                if last:
                    split(U_O2 + 2)
                    mix_split(1, 2)
                act.wait_ge(t_done, 2 * j + 2)
                nc.scalar.activation(bt[:], rg[:], ACT.Sqrt, scale=4.0).then_inc(root_t_done, 1)
                if last:
                    for p in range(3, EARLY + 2):
                        split(U_O2 + p)
                        mix_split(1, p)
                    split(U_O2 + EARLY + 2)
                if not last:
                    for p in (6, 7, 8):
                        next_split(p)

            with act.Fori(0, CHUNKS - 1) as j:
                lru_body(j, False)
            lru_body(CHUNKS - 1, True)
            out_phase(1, U_O2, lambda p, half: None)

        @block.vector
        def _(dve):
            def split_lo(s, u):
                dve.wait_ge(hi_done, u + 1)
                nc.vector.tensor_tensor(w_lo[:, s, :], raw[:, s, :], w_hi[:, s, :].bitcast(F32), ALU.subtract)\
                    .then_inc(lo_done, 1)

            def split(u):
                split_lo(slot(u), u)

            def norm_turned(m, groups=range(4)):
                st = m % ST
                for j in groups:
                    g = 4 * m + j
                    at = u_lo[:, 4 * j:4 * j + 4, st * P:(st + 1) * P]
                    dve.wait_ge(u_hi_done, g + 1)
                    nc.vector.tensor_tensor(at, bank[4 + j][:].rearrange("p (k s) -> p k s", k=4),
                                            u_hi[:, 4 * j:4 * j + 4, st * P:(st + 1) * P].bitcast(F32),
                                            ALU.subtract).then_inc(u_lo_done, 1)

            def reciprocal_root(kind, st, column):
                n = root_count(kind, st)
                rstd = stat[:, 40 + n:41 + n]
                dve.wait_ge(root_done, n)
                nc.vector.reciprocal(rstd, stat[:, column:column + 1]).then_inc(rstd_done, 1)
                dve.wait_ge(rstd_done, n)
                return rstd

            def norm_x(st, parts=range(4)):
                rstd = stat[:, 40 + root_count("x", st):41 + root_count("x", st)]
                if 0 in parts:
                    reciprocal_root("x", st, 2 * st + 1)
                    if st >= 2:
                        dve.wait_ge(u_turned, 4 * (st - 1))
                for j in parts:
                    cols = slice(512 * j, 512 * j + 512)
                    if st == 0:
                        dve.wait_ge(gain_kept, j + 1)
                    nc.vector.scalar_tensor_tensor(out=un[:, st % 2, cols], in0=h[:, st, cols], scalar=rstd,
                                                   in1=gain_pre[:, cols], op0=ALU.mult, op1=ALU.mult)\
                        .then_inc(un_ready, 1)

            nc.vector.memset(stat[:, 126:127], 0.0).then_inc(gate_ready, 1)
            norm_x(0)
            split(U_V)
            norm_turned(0, range(2))
            split(U_V + 1)
            norm_turned(0, range(2, 4))
            split(U_V + 2)
            norm_x(1)
            split(U_V + 3)
            for st in (2, 3):
                norm_turned(st - 1, range(2))
                norm_x(st, range(2))
                norm_turned(st - 1, range(2, 4))
                norm_x(st, range(2, 4))

            def keep_values(b):
                if b < NB - 1:
                    dve.wait_ge(v_proj, b + 1)
                else:
                    dve.wait_ge(weights_used, U_V + 4)
                nc.vector.tensor_scalar(vc[:, b, :], bank[b][:, 0:KV_W], 0.5, None, ALU.mult).then_inc(v_kept, 1)

            norm_turned(3)
            for b in range(NB - 1):
                keep_values(b)
            split(U_K)
            keep_values(NB - 1)
            for j in range(1, 7):
                split(U_K + j)
            dve.wait_ge(weights_used, U_K + 4)
            dve.wait_ge(k_kept, 4)
            for t in range(2):
                for half in range(2):
                    nc.vector.tensor_copy(kc[64 * half:64 * half + 64, 2 * t, :], bank[4 + t][0:64, :])\
                        .then_inc(k_kept, 1)
            lamv = vec[:, LAM:LAM + KT]

            def softplus():
                n = [2]

                def step(ins):
                    n[0] += 1
                    ins.then_inc(soft_step, 1)
                    dve.wait_ge(soft_step, n[0])
                dve.wait_ge(soft_exp, 1)
                z, den, s, s2, acc = (soft[:, i, :] for i in range(1, 6))
                step(nc.vector.tensor_scalar(den, z, 2.0, None, ALU.add))
                step(nc.vector.reciprocal(den, den))
                step(nc.vector.tensor_tensor(s, z, den, ALU.mult))
                step(nc.vector.tensor_tensor(s2, s, s, ALU.mult))
                step(nc.vector.tensor_scalar(acc, s2, 1.0 / 17, 1.0 / 15, ALU.mult, ALU.add))
                for odd in (13, 11, 9, 7, 5, 3, 1):
                    step(nc.vector.tensor_tensor(acc, acc, s2, ALU.mult))
                    step(nc.vector.tensor_scalar(acc, acc, 1.0 / odd, None, ALU.add))
                step(nc.vector.tensor_tensor(acc, acc, s, ALU.mult))
                step(nc.vector.tensor_scalar(z, lamv, -1.0, 0.0, ALU.mult, ALU.max))
                step(nc.vector.scalar_tensor_tensor(out=acc, in0=acc, scalar=2.0, in1=z, op0=ALU.mult, op1=ALU.add))
                step(nc.vector.tensor_scalar(sp4[:], acc, 4.0, None, ALU.mult))

            def kg_build(c, group):
                dve.wait_ge(kg_hi_done, c + 1)
                nc.vector.tensor_tensor(kg_lo[:], kc[:, group, :], kg_hi[:].bitcast(F32), ALU.subtract)\
                    .then_inc(kg_lo_done, 1)

            def v_build(c, group):
                dve.wait_ge(v_hi_done, c + 1)
                nc.vector.tensor_tensor(v_both[:, :, HEAD:P], vc[:, :, ds(group * HEAD, HEAD)],
                                        v_both[:, :, 0:HEAD].bitcast(F32), ALU.subtract).then_inc(v_lo_done, 1)

            def q_kept(c):
                for hd in range(4):
                    high = slice(HEAD * (hd % 2), HEAD * (hd % 2) + HEAD)
                    low = slice(HEAD - HEAD * (hd % 2), 2 * HEAD - HEAD * (hd % 2))
                    dve.wait_ge(q_hi_done, 4 * c + hd + 1)
                    nc.vector.scalar_tensor_tensor(out=q_both[low, hd, :], in0=bank[hd // 2][high, :],
                                                   scalar=HEAD ** -0.5, in1=q_both[high, hd, :].bitcast(F32),
                                                   op0=ALU.mult, op1=ALU.subtract).then_inc(q_lo_done, 1)

            kg_build(0, 0)
            v_build(0, 0)
            split(U_Q + 3)
            dve.wait_ge(vec_turned, 1)
            nc.vector.tensor_copy(vec[:], bank[6][:, 0:P]).then_inc(vec_ready, 1)
            dve.wait_ge(vec_ready, 1)
            nc.vector.scalar_tensor_tensor(out=soft[:, 0, :], in0=lamv, scalar=-1.0, in1=lamv,
                                           op0=ALU.mult, op1=ALU.min).then_inc(soft_step, 1)
            nc.vector.tensor_scalar(nsink[:], nsink[:], -1.0, None, ALU.mult).then_inc(soft_step, 1)
            split(U_Q + 4)
            softplus()
            split(U_Q + 5)
            split(U_Q + 6)
            q_kept(0)

            def mask_max(c, b):
                e = 4 * c + b
                w = P if b == 0 else 2 * P
                buf = b % 2
                dve.wait_ge(scores_done, e + 1)
                for t in range(2):
                    nc.vector.tensor_tensor(
                        probs[:, buf, 2 * t:2 * t + 2, 0:w],
                        bank[4 + t][:].rearrange("p (h k) -> p h k", h=2)[:, :, 0:w],
                        mask[:, 2 * P - w:2 * P].unsqueeze(1).to_broadcast([P, 2, w]), ALU.add)\
                        .then_inc(scores_masked, 1)
                dve.wait_ge(scores_masked, 2 * e + 2)
                nc.vector.tensor_reduce(row_max[:, buf, :], probs[:, buf, :, 0:w], AX_X, ALU.max)\
                    .then_inc(max_done, 1)
                dve.wait_ge(max_done, e + 1)
                nc.vector.scalar_tensor_tensor(out=shift[:, buf, :], in0=row_max[:, buf, :], scalar=-1.0,
                                               in1=nsink[:, ds(4 * c, 4)], op0=ALU.mult, op1=ALU.min)\
                    .then_inc(shift_done, 1)
                dve.wait_ge(shift_done, e + 1)
                nc.vector.tensor_tensor(sink_shift[:, buf, :], shift[:, buf, :], nsink[:, ds(4 * c, 4)],
                                        ALU.subtract).then_inc(sink_shift_done, 1)

            def normalise(c, b):
                e = 4 * c + b
                w = P if b == 0 else 2 * P
                buf = b % 2
                dve.wait_ge(exp_done, 5 * e + 5)
                nc.vector.tensor_tensor(denom[:, buf, :], row_sum[:, buf, :], sink_exp[:, buf, :], ALU.add)\
                    .then_inc(denom_done, 1)
                dve.wait_ge(denom_done, e + 1)
                nc.vector.reciprocal(denom[:, buf, :], denom[:, buf, :]).then_inc(recip_done, 1)
                dve.wait_ge(recip_done, e + 1)
                nc.vector.tensor_tensor(probs[:, buf, :, 0:w], probs[:, buf, :, 0:w],
                                        denom[:, buf, :].unsqueeze(2).to_broadcast([P, 4, w]), ALU.mult)\
                    .then_inc(probs_ready, 1)

            def att_slot(c, s):
                for step in ATT_STEPS.get(s, ()):
                    if step[0] == "T":
                        _, b, k = step
                        dve.wait_ge(pt_hi_done, t_index(c, b, k) + 1)
                        nc.vector.tensor_tensor(pt_lo[:, k, :], bank[6][:], pt_hi[:, k, :].bitcast(F32),
                                                ALU.subtract).then_inc(pt_lo_done, 1)
                    elif step[0] == "V":
                        b = step[1]
                        dve.wait_ge(pv_low_kept, 4 * c + b + 1)
                        for half in range(2):
                            high, low = (at.rearrange("p (t e q) -> p t e q", t=2, e=2)[:, :, half, :]
                                         for at in (bank[7][0:HEAD, :], pv_low[:]))
                            rows = slice(HEAD * half, HEAD * half + HEAD)
                            ins = nc.vector.tensor_tensor(mix[rows, ds(2 * c, 2), b * P:(b + 1) * P], high, low,
                                                          ALU.add)
                        ins.then_inc(pv_read, 1)
                for step in ATT_STEPS.get(s - 2, ()):
                    if step[0] == "S":
                        normalise(c, step[1])
                for step in ATT_STEPS.get(s, ()):
                    if step[0] == "S":
                        mask_max(c, step[1])

            def mix_split(layer, w):
                dve.wait_ge(mix_hi, CHUNKS * layer + w + 1)
                nc.vector.tensor_tensor(u_lo[:, 2 * w:2 * w + 2, :], mix[:, 2 * w:2 * w + 2, :],
                                        u_hi[:, 2 * w:2 * w + 2, :].bitcast(F32), ALU.subtract).then_inc(mix_lo, 1)

            def keep_gate(c):
                for t in range(2):
                    dve.wait_ge(gate_tanh, 2 * c + t + 1)
                    ins = nc.vector.scalar_tensor_tensor(out=gate[:, t, :], in0=gate[:, t, :], scalar=1.0,
                                                         in1=bank[2 + t][:], op0=ALU.add, op1=ALU.mult)
                ins.then_inc(gate_ready, 1)

            def att_body(c, last):
                for s in range(8 if last else 16):
                    att_slot(c, s)
                    if last and s == 7:
                        keep_gate(c)
                    if s in (0, 2, 4, 7, 8, 10, 12, 14):
                        p = s // 2
                        split_lo((p + 3) % DEPTH, U_ATT + 8 * c + p + 3)
                    if last and s in (4, 7):
                        mix_split(0, s // 5)
                    if s == 8:
                        keep_gate(c)
                if not last:
                    kg_build(c + 1, (c + 1) // 2)
                    q_kept(c + 1)
                    v_build(c + 1, (c + 1) // 2)

            with dve.Fori(0, CHUNKS - 1) as c:
                att_body(c, False)
            att_body(CHUNKS - 1, True)

            def copies(layer, st, n):
                y = h if layer == 0 else y2
                dve.wait_ge(o_squared, 16 * layer + 4 * n + st + 1)
                nc.vector.tensor_tensor(y[:, st, ds(512 * n, 512)], bank[st][:], gain_post[:, ds(512 * n, 512)],
                                        ALU.mult).then_inc(o_copied, 1)

            def total(kind, st, first):
                n = root_count(kind, st)
                nc.vector.tensor_reduce(stat[:, 60 + n:61 + n], stat[:, first:first + 4], AX_X, ALU.add)\
                    .then_inc(sum_done, 1)

            def output_total(layer, st):
                dve.wait_ge(o_squared, 16 * layer + 12 + st + 1)
                total("C" if layer else "A", st, 8 + 4 * st)

            def output_root(layer, st):
                kind = "C" if layer else "A"
                return reciprocal_root(kind, st, 80 + root_count(kind, st))

            def residual(layer, st, rstd, parts=range(4)):
                dve.wait_ge(o_copied, 16 * layer + 13 + st)
                if layer == 0:
                    dve.wait_ge(again_landed[st % 2], 16 * (st // 2 + 1))
                for j in parts:
                    cols = slice(512 * j, 512 * j + 512)
                    y = y2[:, st, cols] if layer else h[:, st, cols]
                    other = h[:, st, cols] if layer else x_again[st % 2][:, cols]
                    nc.vector.scalar_tensor_tensor(out=h[:, st, cols], in0=y, scalar=rstd, in1=other,
                                                   op0=ALU.mult, op1=ALU.add).then_inc(h_ready, 1)

            def input_total(st):
                dve.wait_ge(sq_done, ST + 4 * st + 4)
                total("B", st, 100 + 4 * st)

            def next_norm(st, parts=range(4)):
                n = root_count("B", st)
                rstd = stat[:, 40 + n:41 + n]
                if 0 in parts:
                    reciprocal_root("B", st, 80 + n)
                for j in parts:
                    at = un[:, st % 2, 512 * j:512 * j + 512]
                    dve.wait_ge(hg_done, 4 * st + j + 1)
                    nc.vector.tensor_scalar(at, at, rstd, None, ALU.mult).then_inc(un_ready, 1)

            def out_phase(layer, u0, extra):
                for p in range(EARLY * layer, 8):
                    extra(p, 0)
                    if p < 6:
                        mix_split(layer, p + 2)
                    split(u0 + p + 3)
                    extra(p, 1)
                dve.wait_ge(post_landed, 16 * (layer + 1))
                with dve.Fori(1, 3) as n:
                    for p in range(8):
                        if p == 0:
                            for st in range(ST):
                                copies(layer, st, n - 1)
                        split_lo((u0 + p + 3) % DEPTH, u0 + 8 * n + p + 3)
                for p in range(8):
                    if p == 0:
                        for st in range(ST):
                            copies(layer, st, 2)
                    split(u0 + 24 + p + 3)
                first = u0 + 32
                copies(layer, 0, 3)
                copies(layer, 1, 3)
                split(first + 3)
                output_total(layer, 0)
                output_total(layer, 1)
                rstds = [output_root(layer, st) for st in range(2)]
                split(first + 4)
                split(first + 5)
                residual(layer, 0, rstds[0])
                split(first + 6)
                split(first + 7)
                residual(layer, 1, rstds[1])
                if layer == 0:
                    input_total(0)
                    next_norm(0)
                    split(U_LRU)
                    input_total(1)
                    next_norm(1)
                    norm_turned(ST)
                copies(layer, 2, 3)
                output_total(layer, 2)
                if layer == 0:
                    norm_turned(ST + 1)
                rstd = output_root(layer, 2)
                if layer == 1:
                    residual(layer, 2, rstd)
                    copies(layer, 3, 3)
                    output_total(layer, 3)
                    residual(layer, 3, output_root(layer, 3), range(3))
                    return
                split(U_LRU + 1)
                residual(layer, 2, rstd, range(2))
                split(U_LRU + 2)
                residual(layer, 2, rstd, range(2, 4))
                copies(layer, 3, 3)
                output_total(layer, 3)
                input_total(2)
                split(U_LRU + 3)
                residual(layer, 3, output_root(layer, 3))
                next_norm(2, range(2))
                input_total(3)
                next_norm(2, range(2, 4))
                next_norm(3)
                norm_turned(ST + 2)
                norm_turned(ST + 3)

            def att_tail(p, half):
                att_slot(CHUNKS - 1, 8 + 2 * p + half)

            out_phase(0, U_O1, att_tail)

            for p in range(1, 3):
                split(U_LRU + p + 3)

            def lru_body(j, last):
                def next_split(p):
                    split_lo((4 + p + 2) % LRU_DEPTH if not last else slot(U_LRU + 4 + 9 * j + p + 2),
                             U_LRU + 4 + 9 * j + p + 2)

                dve.wait_ge(conv_begun, 2 * j + 2)
                for back in (1, 2, 3):
                    if back > 1:
                        dve.wait_ge(conv_tap, 6 * j + 2 * back - 2)
                    for t in range(2):
                        nc.vector.scalar_tensor_tensor(
                            out=xc[:, t, back:SEQ], in0=bank[t][:, 0:SEQ - back],
                            scalar=vec[:, ds(CONV_W + (3 - back) * KT + 2 * j + t, 1)], in1=xc[:, t, back:SEQ],
                            op0=ALU.mult, op1=ALU.add).then_inc(conv_tap, 1)
                next_split(0)
                dve.wait_ge(xc_hi_done, j + 1)
                nc.vector.tensor_tensor(xc_lo[:], xc[:], xc_hi[:].bitcast(F32), ALU.subtract).then_inc(xc_lo_done, 1)
                for p in (1, 2, 3):
                    next_split(p)
                silu = lgate_last if last else lgate
                for t in range(2):
                    dve.wait_ge(lgate_tanh, 2 * j + t + 1)
                    nc.vector.scalar_tensor_tensor(out=silu[:, t, :], in0=silu[:, t, :], scalar=1.0,
                                                   in1=bank[2 + t][:], op0=ALU.add, op1=ALU.mult)\
                        .then_inc(lgate_ready, 1)
                next_split(4)
                if last:
                    for w in range(2):
                        mix_split(1, w)
                dve.wait_ge(t_done, 2 * j + 2)
                nc.vector.tensor_scalar(decay[:], rg[:], 1.0, None, ALU.add).then_inc(one_plus_t, 1)
                if last:
                    split(U_O2 + 2)
                    mix_split(1, 2)
                else:
                    next_split(5)
                dve.wait_ge(one_plus_t, j + 1)
                for t in range(2):
                    nc.vector.reciprocal(decay[:, t, :], decay[:, t, :]).then_inc(q_recip, 1)
                    if last:
                        split(U_O2 + t + 3)
                        mix_split(1, t + 3)
                    elif t == 0:
                        next_split(6)
                dve.wait_ge(q_recip, 2 * j + 2)
                dve.wait_ge(root_t_done, j + 1)
                nc.vector.tensor_tensor(bt[:], bt[:], decay[:], ALU.mult).then_inc(b_step, 1)
                dve.wait_ge(b_step, 2 * j + 1)
                nc.vector.tensor_scalar(decay[:], decay[:], 2.0, -1.0, ALU.mult, ALU.add).then_inc(a_done, 1)
                if last:
                    split(U_O2 + EARLY + 2)
                else:
                    next_split(7)
                dve.wait_ge(ix_done, j + 2)
                nc.vector.tensor_tensor(bt[:], bt[:], ig[:], ALU.mult).then_inc(b_step, 1)
                dve.wait_ge(a_done, j + 1)
                dve.wait_ge(b_step, 2 * j + 2)
                for t in range(2):
                    nc.vector.tensor_tensor_scan(rg[:, t, :], decay[:, t, :], bt[:, t, :], 0.0, ALU.mult, ALU.add)\
                        .then_inc(scan_done, 1)
                if not last:
                    next_split(8)
                dve.wait_ge(scan_done, 2 * j + 2)
                dve.wait_ge(lgate_ready, 2 * j + 2)
                nc.vector.scalar_tensor_tensor(out=mix[:, ds(2 * j, 2), :], in0=rg[:], scalar=0.5, in1=silu[:],
                                               op0=ALU.mult, op1=ALU.mult).then_inc(lmix_ready, 1)

            with dve.Fori(0, CHUNKS - 1) as j:
                lru_body(j, False)
            lru_body(CHUNKS - 1, True)
            out_phase(1, U_O2, lambda p, half: None)

        @block.tensor
        def _(pe):
            def weights(s):
                return (w_hi[:, s, :].rearrange("p (k n) -> p k n", n=256),
                        w_lo[:, s, :].rearrange("p (k n) -> p k n", n=256))

            def three(out_ap, lhs_hi, lhs_lo, rhs_hi, rhs_lo, start, stop, shared=False):
                pe.matmul(out_ap, lhs_hi, rhs_hi, start=start, stop=False, skip_group_check=shared)
                pe.matmul(out_ap, lhs_hi, rhs_lo, start=False, stop=False, skip_group_check=shared)
                return pe.matmul(out_ap, lhs_lo, rhs_hi, start=False, stop=stop, skip_group_check=shared)

            def project_half(s, part, tile, half):
                hi, lo = weights(s)
                tokens = slice(256 * half, 256 * half + 256)
                for kk in range(4):
                    kt = 4 * part + kk
                    cols = slice(tile * P, (tile + 1) * P)
                    ins = three(bank[tile][:, tokens], hi[:, kk, cols], lo[:, kk, cols], u_hi[:, kt, tokens],
                                u_lo[:, kt, tokens], kt == 0 and half == 0, kt == KT - 1 and half == 1,
                                shared=True)
                return ins

            def project(s, part, banks, tile):
                hi, lo = weights(s)
                for kk in range(4):
                    kt = 4 * part + kk
                    cols = slice(tile * P, (tile + 1) * P)
                    ins = three(bank[banks + tile][:], hi[:, kk, cols], lo[:, kk, cols], u_hi[:, kt, :],
                                u_lo[:, kt, :], kt == 0, kt == KT - 1)
                return ins

            def turn(m, groups=range(4)):
                for j in groups:
                    g = 4 * m + j
                    pe.wait_ge(un_ready, g + 1)
                    if g >= 4:
                        pe.wait_ge(u_lo_done, g - 3)
                    for k in range(4):
                        ins = pe.transpose(bank[4 + j][:, k * P:(k + 1) * P],
                                           un[:, m % 2, (4 * j + k) * P:(4 * j + k + 1) * P], ident[:])
                    ins.then_inc(u_turned, 1)

            pe.wait_ge(consts_ready, 7)
            pe.wait_ge(row_landed, 16)
            for j in range(4):
                pe.matmul(bank[j][:], ones_row[:], gain_row[:, 512 * j:512 * j + 512], start=True, stop=True)\
                    .then_inc(gain_spread, 1)
            turn(0)
            pe.wait_ge(gain_kept, 4)
            for st in range(ST):
                cols = slice(st * P, (st + 1) * P)
                for j in range(4):
                    pe.wait_ge(u_lo_done, 4 * st + j + 1)
                    pe.wait_ge(lo_done, U_V + j + 1)
                    hi, lo = weights(slot(U_V + j))
                    for kk in range(4):
                        kt = 4 * j + kk
                        ins = three(bank[st][:, 0:KV_W], u_hi[:, kt, cols], u_lo[:, kt, cols], hi[:, kk, :],
                                    lo[:, kk, :], kt == 0, kt == KT - 1)
                    if st == ST - 1:
                        ins.then_inc(weights_used, 1)
                    elif j == 3:
                        ins.then_inc(v_proj, 1)
                    if j and st < ST - 1:
                        turn(st + 1, range(j - 1, j) if j < 3 else range(2, 4))
            for j in range(4):
                pe.wait_ge(lo_done, U_K + j + 1)
                for tile in range(2):
                    ins = project(slot(U_K + j), j, 4, tile)
                ins.then_inc(weights_used, 1)
            pe.wait_ge(small_landed, 16 * 6)
            pe.transpose(bank[6][:, 0:P], vec_rows[:], ident[:]).then_inc(vec_turned, 1)
            pe.wait_ge(v_kept, 4)
            for j in range(4):
                pe.wait_ge(lo_done, U_Q + j + 1)
                for tile in range(2):
                    ins = project(slot(U_Q + j), j, 0, tile)
                    if tile:
                        ins.then_inc(weights_used, 1)
                    elif j == 3:
                        ins.then_inc(q_proj, 1)

            def scores(c, b):
                k0 = max(b - 1, 0) * P
                if b == 0:
                    pe.wait_ge(q_lo_done, 4 * c + 4)
                    pe.wait_ge(kg_lo_done, c + 1)
                    pe.wait_ge(vec_ready, 1)
                else:
                    pe.wait_ge(scores_masked, 2 * (4 * c + b))
                for hd in range(4):
                    q = q_both[:, hd, b * P:(b + 1) * P]
                    at = bank[4 + hd // 2][:, 2 * P * (hd % 2):2 * P * (hd % 2) + 2 * P]
                    pe.matmul(at, q, kg_hi[:, k0:k0 + 2 * P], start=True, stop=False)
                    ins = pe.matmul(at, q, kg_lo[:, k0:k0 + 2 * P], start=False, stop=True)
                ins.then_inc(scores_done, 1)

            def turn_probs(c, b, k):
                if b == 0 or k == 0:
                    pe.wait_ge(probs_ready, 4 * c + b + 1)
                if b:
                    pe.wait_ge(pt_lo_done, t_index(c, b, k))
                at = 0 if b == 0 else k * P
                for hd in range(4):
                    ins = pe.transpose(bank[6][:, hd * P:(hd + 1) * P], probs[:, b % 2, hd, at:at + P], ident[:])
                ins.then_inc(p_turned, 1)

            def weigh_values(c, b):
                if b == 0:
                    pe.wait_ge(v_lo_done, c + 1)
                    pe.wait_ge(mix_ready, c + 1)
                else:
                    pe.wait_ge(pv_read, 4 * c + b)
                pe.wait_ge(pt_lo_done, t_index(c, b, 1) + 1)
                for k in ((1,) if b == 0 else (0, 1)):
                    kb = b - 1 + k
                    pe.matmul(bank[7][:], v_both[:, kb, :], pt_hi[:, k, :], start=b == 0 or k == 0, stop=False)
                    ins = pe.matmul(bank[7][:], v_both[:, kb, :], pt_lo[:, k, :], start=False, stop=k == 1)
                ins.then_inc(pv_done, 1)

            def att_slot(c, s):
                for step in ATT_STEPS.get(s, ()):
                    if step[0] == "S":
                        scores(c, step[1])
                    elif step[0] == "T":
                        turn_probs(c, step[1], step[2])
                    else:
                        weigh_values(c, step[1])

            def att_body(c, last):
                for p in range(4 if last else 8):
                    pe.wait_ge(lo_done, U_ATT + 8 * c + p + 1)
                    gates = p < 4
                    if p == 0:
                        pe.wait_ge(gate_ready, c + 1)
                    if p == 4:
                        pe.wait_ge(q_lo_done, 4 * c + 4)
                    for tile in range(2):
                        ins = project(p % DEPTH, p % 4, 2 if gates else 0, tile)
                        if tile:
                            ins.then_inc(weights_used, 1)
                        elif p % 4 == 3:
                            ins.then_inc(gate_proj if gates else q_proj, 1)
                        att_slot(c, 2 * p + tile)

            with pe.Fori(0, CHUNKS - 1) as c:
                att_body(c, False)
            att_body(CHUNKS - 1, True)

            def out_unit(s, p, tiles, done, last_use=True):
                hi = w_hi[:, s, :].rearrange("p (k n) -> p k n", n=512)
                lo = w_lo[:, s, :].rearrange("p (k n) -> p k n", n=512)
                for st in tiles:
                    cols = slice(st * P, (st + 1) * P)
                    for kk in range(2):
                        kt = 2 * p + kk
                        ins = three(bank[st][:], u_hi[:, kt, cols], u_lo[:, kt, cols], hi[:, kk, :], lo[:, kk, :],
                                    kt == 0, kt == KT - 1)
                    if st == tiles[-1] and last_use:
                        ins.then_inc(weights_used, 1)
                    elif p == 7:
                        ins.then_inc(o_done, 1)
                    done(st)

            def out_phase(layer, u0):
                b0 = 16 * layer
                for p in range(8):
                    pe.wait_ge(lo_done, u0 + p + 1)
                    pe.wait_ge(mix_lo, CHUNKS * layer + p + 1)

                    def attention(st, p=p):
                        if layer == 0 and st % 2 and p < 4:
                            att_slot(CHUNKS - 1, 8 + 2 * p + st // 2)
                        if layer == 0 and p == 0 and st == 1:
                            pe.wait_ge(gate_ready, CHUNKS + 1)
                    out_unit((u0 + p) % DEPTH, p, range(ST), attention)
                with pe.Fori(1, 3) as n:
                    for p in range(8):
                        pe.wait_ge(lo_done, u0 + 8 * n + p + 1)

                        if p == 0:
                            pe.wait_ge(o_copied, b0 + 4 * n - 3)

                        def copied(st, p=p):
                            if p == 0 and st < ST - 1:
                                pe.wait_ge(o_copied, b0 + 4 * n - 3 + st + 1)
                        out_unit((u0 + p) % DEPTH, p, range(ST), copied)
                for half in range(2):
                    for p in range(8 if half == 0 else TOGETHER):
                        pe.wait_ge(lo_done, u0 + 24 + 8 * half + p + 1)
                        if p == 0:
                            pe.wait_ge(o_copied, b0 + 10 + 2 * half)
                        out_unit((u0 + p) % DEPTH, p, range(2 * half, 2 * half + 2), lambda st: None)
                for p in range(TOGETHER, 8):
                    pe.wait_ge(lo_done, u0 + 32 + p + 1)
                    out_unit((u0 + p) % DEPTH, p, [2], lambda st: None, last_use=False)
                if layer == 0:
                    turn(ST)
                for p in range(TOGETHER, 8):
                    out_unit((u0 + p) % DEPTH, p, [3], lambda st: None)
                    if layer == 0 and p == 6:
                        turn(ST + 1)

            pe.wait_ge(q_lo_done, 4 * CHUNKS)
            out_phase(0, U_O1)

            for j in range(4):
                pe.wait_ge(u_lo_done, 4 * (ST + 1) + j + 1)
                pe.wait_ge(lo_done, U_LRU + j + 1)
                for tile in range(2):
                    project_half(slot(U_LRU + j), j, tile, 0)
            turn(ST + 2)
            turn(ST + 3)
            for j in range(4):
                pe.wait_ge(u_lo_done, 4 * (2 * ST - 1) + j + 1)
                for tile in range(2):
                    ins = project_half(slot(U_LRU + j), j, tile, 1)
                    if tile:
                        ins.then_inc(weights_used, 1)
                    elif j == 3:
                        ins.then_inc(xb_proj, 1)

            def lru_body(j, last):
                for p in range(5 if last else 9):
                    s = (4 + p) % LRU_DEPTH
                    pe.wait_ge(lo_done, U_LRU + 4 + 9 * j + p + 1)
                    if p == 4:
                        pe.wait_ge(xc_lo_done, j + 1)
                        hi, lo = weights(s)
                        for g in range(2):
                            for tile in range(2):
                                cols = slice(tile * P, (tile + 1) * P)
                                for kk in range(2):
                                    ins = three(bank[4 + 2 * g + tile][:], hi[:, 2 * g + kk, cols],
                                                lo[:, 2 * g + kk, cols], xc_hi[:, kk, :], xc_lo[:, kk, :],
                                                kk == 0, kk == 1)
                                if g and tile:
                                    ins.then_inc(weights_used, 1)
                                else:
                                    ins.then_inc(ri_proj, 1)
                        continue
                    gates = p < 4
                    if p == 5:
                        pe.wait_ge(conv_tap, 6 * j + 6)
                    for tile in range(2):
                        ins = project(s, p if gates else p - 5, 2 if gates else 0, tile)
                        if tile:
                            ins.then_inc(weights_used, 1)
                        elif p in (3, 8):
                            ins.then_inc(lgate_proj if gates else xb_proj, 1)
                pe.wait_ge(lgate_ready, 2 * j + 2)

            with pe.Fori(0, CHUNKS - 1) as j:
                lru_body(j, False)
            lru_body(CHUNKS - 1, True)
            pe.wait_ge(conv_tap, 6 * CHUNKS)
            out_phase(1, U_O2)


def program(nc, a, out):
    rows = lambda ap, spec, **k: ap.rearrange(spec, **k)
    build(
        nc,
        rows(a["x"], "b s d -> (b s) d"), a["norm_pre"], a["norm_post"],
        rows(a["attn_w_in"], "a k n -> (a k) n"), rows(a["attn_w_out"], "a k n -> (a k) n"), a["attn_sinks"],
        rows(a["lru_w_in"], "a k n -> (a k) n"),
        rows(a["lru_conv_w"], "a c (t p) -> (a c t) p", p=P), rows(a["lru_conv_b"], "a (t p) -> (a t) p", p=P),
        rows(a["lru_w_a"], "a g i o -> (a g i) o"), rows(a["lru_b_a"], "a g (t p) -> (a g t) p", p=P),
        rows(a["lru_w_x"], "a g i o -> (a g i) o"), rows(a["lru_b_x"], "a g (t p) -> (a g t) p", p=P),
        rows(a["lru_lambda"], "a (t p) -> (a t) p", p=P),
        rows(a["lru_w_out"], "a k n -> (a k) n"),
        rows(out, "b s d -> (b s) d"),
    )


INPUTS = ["x", "norm_pre", "norm_post", "attn_w_in", "attn_w_out", "attn_sinks", "lru_w_in", "lru_conv_w",
          "lru_conv_b", "lru_w_a", "lru_b_a", "lru_w_x", "lru_b_x", "lru_lambda", "lru_w_out"]


def kernel(**inputs):
    import numpy as np
    import concourse.bacc as bacc
    from concourse.bass_utils import run_bass_kernel_spmd

    nc = bacc.Bacc("TRN2", target_bir_lowering=False, num_devices=1)
    arrays, args = {}, {}
    for name in INPUTS:
        a = np.ascontiguousarray(inputs[name])
        arrays[f"in_{name}"] = a
        args[name] = nc.dram_tensor(f"in_{name}", a.shape, mybir.dt.from_np(a.dtype), kind="ExternalInput").ap()
    out = nc.dram_tensor("out", (1, SEQ, D), F32, kind="ExternalOutput").ap()
    program(nc, args, out)
    return run_bass_kernel_spmd(nc, [arrays], core_ids=[0]).results[0]["out"]
```
